# Optimizing a Trainium2 kernel written in Bass

```python
import math
import jax, jax.numpy as jnp
from jax import lax
import numpy as np

D_MODEL = 1024
BATCH = 1
SEQ = 2048
DEPTH = 2
DEC_BATCH = 8
DEC_SEQ = 8
PAST_LEN = 1024
PAGE_SIZE = 128

N_MIXERS = 2
N_A_LAYERS = (DEPTH + 1) // 2
N_B_LAYERS = DEPTH // 2
GLA_HEADS = 4
GLA_DK = D_MODEL // 2 // GLA_HEADS
GLA_DV = D_MODEL // GLA_HEADS
GLA_LOWRANK = 16
GLA_TAU = 16.0
GLA_CHUNK = 32
GLA_IN = 2 * GLA_HEADS * GLA_DK + 2 * GLA_HEADS * GLA_DV + GLA_LOWRANK
DIFF_HEADS = 8
DIFF_DH = D_MODEL // DIFF_HEADS // 2
DIFF_VD = 2 * DIFF_DH
DIFF_WIDTH = DIFF_HEADS * DIFF_VD
Q_BLOCK = 128
N_BUCKETS = 32
MAX_DISTANCE = 128
PLE_DIM = 256
ALPHA = (2 * DEPTH) ** 0.25
BETA = (8 * DEPTH) ** -0.25
N_PAGES = PAST_LEN // PAGE_SIZE
N_POOL = (DEC_BATCH * N_PAGES * 5) // 4
EPS = 1e-5

kernel_name = 'hybrid_gla_diffattn_decoder'

F32 = jnp.float32

def layer_norm(x, g, b):
    xf = x.astype(F32)
    mu = jnp.mean(xf, axis=-1, keepdims=True)
    var = jnp.mean(jnp.square(xf - mu), axis=-1, keepdims=True)
    return ((xf - mu) * lax.rsqrt(var + EPS) * g.astype(F32) + b.astype(F32)).astype(x.dtype)

def head_rmsnorm(o, g):
    of = o.astype(F32)
    of = of * lax.rsqrt(jnp.mean(jnp.square(of), axis=-1, keepdims=True) + EPS)
    return of * g.astype(F32).reshape(o.shape[-2:])

def gla_recurrence(q, k, v, log_a, s0):
    bsz, t, h, _ = q.shape
    dv = v.shape[-1]
    c = math.gcd(t, GLA_CHUNK)
    n = t // c

    def chunks(a):
        return a.astype(F32).reshape(bsz, n, c, h, a.shape[-1])

    q, k, v, log_a = chunks(q), chunks(k), chunks(v), chunks(log_a)
    cum = jnp.cumsum(log_a, axis=2)
    tot = cum[:, :, -1]
    q_dec = q * jnp.exp(cum)
    k_inv = k * jnp.exp(-cum)
    k_end = k * jnp.exp(tot[:, :, None] - cum)
    causal = jnp.tril(jnp.ones((c, c), dtype=bool))
    att = jnp.einsum('bnihd,bnjhd->bnhij', q_dec, k_inv)
    att = jnp.where(causal, att, 0.0)
    o_intra = jnp.einsum('bnhij,bnjhv->bnihv', att, v)

    def step(s, xs):
        qn, kn, vn, tn = xs
        o = jnp.einsum('bihd,bhdv->bihv', qn, s)
        s = jnp.exp(tn)[..., None] * s + jnp.einsum('bjhd,bjhv->bhdv', kn, vn)
        return s, o

    xs = (jnp.moveaxis(q_dec, 1, 0), jnp.moveaxis(k_end, 1, 0), jnp.moveaxis(v, 1, 0), jnp.moveaxis(tot, 1, 0))
    s_final, o_inter = lax.scan(step, s0.astype(F32), xs)
    o = o_intra + jnp.moveaxis(o_inter, 0, 1)
    return o.reshape(bsz, t, h, dv), s_final

def gla_mixer(x, s0, w_in, w_a2, b_a, norm_g, w_out):
    bsz, t, _ = x.shape
    hk = GLA_HEADS * GLA_DK
    hv = GLA_HEADS * GLA_DV
    proj = x @ w_in
    q, k, v, gate, a_lr = jnp.split(proj, [hk, 2 * hk, 2 * hk + hv, 2 * hk + 2 * hv], axis=-1)
    q = q.reshape(bsz, t, GLA_HEADS, GLA_DK) * (GLA_DK ** -0.5)
    k = k.reshape(bsz, t, GLA_HEADS, GLA_DK)
    v = v.reshape(bsz, t, GLA_HEADS, GLA_DV)
    log_a = jax.nn.log_sigmoid((a_lr @ w_a2 + b_a).astype(F32)) / GLA_TAU
    log_a = log_a.reshape(bsz, t, GLA_HEADS, GLA_DK)
    o, s = gla_recurrence(q, k, v, log_a, s0)
    o = head_rmsnorm(o, norm_g).reshape(bsz, t, hv) * jax.nn.silu(gate.astype(F32))
    return o.astype(x.dtype) @ w_out, s

def t5_bucket(rel):
    n = jnp.maximum(rel, 0)
    max_exact = N_BUCKETS // 2
    nf = jnp.maximum(n, 1).astype(F32)
    large = max_exact + (jnp.log(nf / max_exact) / math.log(MAX_DISTANCE / max_exact)
                         * (N_BUCKETS - max_exact)).astype(jnp.int32)
    large = jnp.minimum(large, N_BUCKETS - 1)
    return jnp.where(n < max_exact, n, large)

def diff_lambda(lq1, lk1, lq2, lk2, lam_init):
    return (jnp.exp(jnp.sum(lq1.astype(F32) * lk1.astype(F32)))
            - jnp.exp(jnp.sum(lq2.astype(F32) * lk2.astype(F32))) + lam_init)

def diff_attend(q, k, v, q_pos, k_pos, rel_bias, lam):
    bsz, tq, h, _ = q.shape
    tk = k.shape[1]
    qs = q.reshape(bsz, tq, h, 2, DIFF_DH)
    ks = k.reshape(bsz, tk, h, 2, DIFF_DH)
    s = jnp.einsum('bqhmd,bkhmd->bhmqk', qs, ks).astype(F32) * (DIFF_DH ** -0.5)
    rel = q_pos[:, None] - k_pos[None, :]
    bias = jnp.moveaxis(rel_bias.astype(F32)[t5_bucket(rel)], -1, 0)
    s = s + bias[None, :, None]
    s = jnp.where(rel >= 0, s, jnp.finfo(F32).min)
    p = jax.nn.softmax(s, axis=-1)
    a = p[:, :, 0] - lam * p[:, :, 1]
    return jnp.einsum('bhqk,bkhd->bqhd', a, v.astype(F32))

def diff_project(x, w_in):
    bsz, t, _ = x.shape
    q, k, v, gate = jnp.split(x @ w_in, 4, axis=-1)
    shp = (bsz, t, DIFF_HEADS, DIFF_VD)
    return q.reshape(shp), k.reshape(shp), v.reshape(shp), gate

def diff_output(o, gate, norm_g, lam_init, w_out, dtype):
    bsz, t = o.shape[:2]
    o = head_rmsnorm(o, norm_g) * (1.0 - lam_init)
    o = o.reshape(bsz, t, DIFF_WIDTH) * jax.nn.silu(gate.astype(F32))
    return o.astype(dtype) @ w_out

def diff_prompt(x, w_in, norm_g, w_out, rel_bias, lam, lam_init):
    bsz, t, _ = x.shape
    q, k, v, gate = diff_project(x, w_in)
    qb = math.gcd(t, Q_BLOCK)
    nb = t // qb
    pos = jnp.arange(t, dtype=jnp.int32)
    q_blocks = jnp.moveaxis(q.reshape(bsz, nb, qb, DIFF_HEADS, DIFF_VD), 1, 0)
    pos_blocks = pos.reshape(nb, qb)
    o = lax.map(lambda xs: diff_attend(xs[0], k, v, xs[1], pos, rel_bias, lam), (q_blocks, pos_blocks))
    o = jnp.moveaxis(o, 0, 1).reshape(bsz, t, DIFF_HEADS, DIFF_VD)
    return diff_output(o, gate, norm_g, lam_init, w_out, x.dtype), k, v

def diff_sample(x, cache_k, cache_v, j, page_table, w_in, norm_g, w_out, rel_bias, lam, lam_init):
    bsz, t, _ = x.shape
    q, k, v, gate = diff_project(x, w_in)
    past = page_table.shape[1] * PAGE_SIZE
    k_past = cache_k[j, page_table].reshape(bsz, past, DIFF_HEADS, DIFF_VD)
    v_past = cache_v[j, page_table].reshape(bsz, past, DIFF_HEADS, DIFF_VD)
    k_all = jnp.concatenate([k_past, k.astype(k_past.dtype)], axis=1)
    v_all = jnp.concatenate([v_past, v.astype(v_past.dtype)], axis=1)
    q_pos = past + jnp.arange(t, dtype=jnp.int32)
    k_pos = jnp.arange(past + t, dtype=jnp.int32)
    o = diff_attend(q, k_all, v_all, q_pos, k_pos, rel_bias, lam)
    return diff_output(o, gate, norm_g, lam_init, w_out, x.dtype), k, v

def residual_update(x, f, g, b, p, w_proj, w_gate):
    h = layer_norm(ALPHA * x + f, g, b)
    gate = jax.nn.sigmoid((h @ w_gate).astype(F32))
    return (h.astype(F32) + gate * (p @ w_proj).astype(F32)).astype(x.dtype)

def setup_inputs(seed: int = 0) -> dict:
    key = jax.random.key(seed)
    ks = jax.random.split(key, 26)
    nrm = jax.random.normal
    hk = GLA_HEADS * GLA_DK
    hv = GLA_HEADS * GLA_DV
    perm = jax.random.permutation(ks[5], N_POOL)[:DEC_BATCH * N_PAGES]
    return {
        'x_prompt': nrm(ks[0], (BATCH, SEQ, D_MODEL), F32),
        'x_sample': nrm(ks[1], (DEC_BATCH, DEC_SEQ, D_MODEL), F32),
        'state_gla': 0.5 * nrm(ks[2], (N_A_LAYERS, DEC_BATCH, GLA_HEADS, GLA_DK, GLA_DV), F32),
        'cache_k': nrm(ks[3], (N_B_LAYERS, N_POOL, PAGE_SIZE, DIFF_HEADS, DIFF_VD), F32),
        'cache_v': nrm(ks[4], (N_B_LAYERS, N_POOL, PAGE_SIZE, DIFF_HEADS, DIFF_VD), F32),
        'page_table': perm.reshape(DEC_BATCH, N_PAGES).astype(jnp.int32),
        'p_prompt': nrm(ks[6], (DEPTH, BATCH, SEQ, PLE_DIM), F32),
        'p_sample': nrm(ks[7], (DEPTH, DEC_BATCH, DEC_SEQ, PLE_DIM), F32),
        'rel_bias': 0.5 * nrm(ks[8], (N_BUCKETS, DIFF_HEADS), F32),
        'gla_w_in': nrm(ks[9], (N_A_LAYERS, D_MODEL, GLA_IN), F32) * D_MODEL ** -0.5,
        'gla_w_a2': nrm(ks[10], (N_A_LAYERS, GLA_LOWRANK, hk), F32) * GLA_LOWRANK ** -0.5,
        'gla_b_a': 0.1 * nrm(ks[11], (N_A_LAYERS, hk), F32),
        'gla_norm_g': 1.0 + 0.02 * nrm(ks[12], (N_A_LAYERS, hv), F32),
        'gla_w_out': nrm(ks[13], (N_A_LAYERS, hv, D_MODEL), F32) * (hv ** -0.5 * BETA),
        'diff_w_in': nrm(ks[14], (N_B_LAYERS, D_MODEL, 4 * DIFF_WIDTH), F32) * D_MODEL ** -0.5,
        'diff_lam_q1': 0.1 * nrm(ks[15], (N_B_LAYERS, DIFF_DH), F32),
        'diff_lam_k1': 0.1 * nrm(ks[16], (N_B_LAYERS, DIFF_DH), F32),
        'diff_lam_q2': 0.1 * nrm(ks[17], (N_B_LAYERS, DIFF_DH), F32),
        'diff_lam_k2': 0.1 * nrm(ks[18], (N_B_LAYERS, DIFF_DH), F32),
        'diff_norm_g': 1.0 + 0.02 * nrm(ks[19], (N_B_LAYERS, DIFF_WIDTH), F32),
        'diff_w_out': nrm(ks[20], (N_B_LAYERS, DIFF_WIDTH, D_MODEL), F32) * (DIFF_WIDTH ** -0.5 * BETA),
        'ln_g': 1.0 + 0.02 * nrm(ks[21], (DEPTH, D_MODEL), F32),
        'ln_b': 0.02 * nrm(ks[22], (DEPTH, D_MODEL), F32),
        'ple_w_proj': nrm(ks[23], (DEPTH, PLE_DIM, D_MODEL), F32) * PLE_DIM ** -0.5,
        'ple_w_gate': nrm(ks[24], (DEPTH, D_MODEL, D_MODEL), F32) * D_MODEL ** -0.5,
    }

def reference(x_prompt, x_sample, state_gla, cache_k, cache_v, page_table, p_prompt, p_sample,
              rel_bias, gla_w_in, gla_w_a2, gla_b_a, gla_norm_g, gla_w_out,
              diff_w_in, diff_lam_q1, diff_lam_k1, diff_lam_q2, diff_lam_k2, diff_norm_g, diff_w_out,
              ln_g, ln_b, ple_w_proj, ple_w_gate):
    xp, xs = x_prompt, x_sample
    gla_sp, gla_ss, k_p, v_p, k_s, v_s = [], [], [], [], [], []
    for i in range(DEPTH):
        j = i // N_MIXERS
        if i % N_MIXERS == 0:
            s_zero = jnp.zeros((xp.shape[0], GLA_HEADS, GLA_DK, GLA_DV), F32)
            fp, sp = gla_mixer(xp, s_zero, gla_w_in[j], gla_w_a2[j], gla_b_a[j], gla_norm_g[j], gla_w_out[j])
            fs, ss = gla_mixer(xs, state_gla[j], gla_w_in[j], gla_w_a2[j], gla_b_a[j], gla_norm_g[j], gla_w_out[j])
            gla_sp.append(sp.astype(state_gla.dtype))
            gla_ss.append(ss.astype(state_gla.dtype))
        else:
            lam_init = 0.8 - 0.6 * math.exp(-0.3 * i)
            lam = diff_lambda(diff_lam_q1[j], diff_lam_k1[j], diff_lam_q2[j], diff_lam_k2[j], lam_init)
            fp, kn, vn = diff_prompt(xp, diff_w_in[j], diff_norm_g[j], diff_w_out[j], rel_bias, lam, lam_init)
            fs, kn2, vn2 = diff_sample(xs, cache_k, cache_v, j, page_table, diff_w_in[j], diff_norm_g[j],
                                       diff_w_out[j], rel_bias, lam, lam_init)
            k_p.append(kn.astype(cache_k.dtype))
            v_p.append(vn.astype(cache_v.dtype))
            k_s.append(kn2.astype(cache_k.dtype))
            v_s.append(vn2.astype(cache_v.dtype))
        xp = residual_update(xp, fp, ln_g[i], ln_b[i], p_prompt[i], ple_w_proj[i], ple_w_gate[i])
        xs = residual_update(xs, fs, ln_g[i], ln_b[i], p_sample[i], ple_w_proj[i], ple_w_gate[i])
    return (xp, xs, jnp.stack(gla_sp), jnp.stack(gla_ss), jnp.stack(k_p), jnp.stack(v_p), jnp.stack(k_s), jnp.stack(v_s))


_drawn_inputs = setup_inputs


def setup_inputs(seed=0):
    import zlib

    import numpy as np

    out = dict(_drawn_inputs(seed))
    spreads = {}
    factors = {'gla_norm_g': 8.0,
     'diff_lam_q1': 8.0,
     'diff_lam_k1': 8.0,
     'diff_lam_q2': 8.0,
     'diff_lam_k2': 8.0,
     'diff_norm_g': 8.0}
    for name, (base, spread) in spreads.items():
        noise = np.random.default_rng([zlib.crc32(name.encode()), seed]).standard_normal(out[name].shape)
        drawn = base * np.exp(spread * noise) if base else spread * noise
        out[name] = __import__('jax').numpy.asarray(drawn.astype(out[name].dtype))
    for name, factor in factors.items():
        out[name] = (out[name] * factor).astype(out[name].dtype)
    return out
```

```python
import math
from contextlib import ExitStack

import numpy as np

import concourse.bass as bass
from concourse import mybir

F32 = mybir.dt.float32
F32R = mybir.dt.float32r
I32 = mybir.dt.int32
ALU = mybir.AluOpType
ACT = mybir.ActivationFunctionType
AX = mybir.AxisListType

P = 128
D = 1024
KD = D // P
SEQ = 2048
DEC_BATCH = 8
DEC_SEQ = 8
SAMPLE_ROWS = DEC_BATCH * DEC_SEQ
PROMPT_TILES = SEQ // P
TILES = PROMPT_TILES + 1
ROWS = TILES * P
BANK = 512
EPS = 1e-5
DEPTH = 2
ALPHA = (2 * DEPTH) ** 0.25
PLE = 256
KP = PLE // P

G_HEADS, G_DK, G_DV = 4, 128, 256
G_LOW = 16
G_TAU = 16.0
G_CHUNK = 32
CHUNKS = P // G_CHUNK
GK = G_HEADS * G_DK
GV = G_HEADS * G_DV

D_HEADS, D_DH, D_VD = 8, 64, 128
N_BUCKETS = 32
MAX_DISTANCE = 128
PAGE = 128
N_PAGES = 8
N_POOL = 80
PAST = PAGE * N_PAGES
LAM_INIT = 0.8 - 0.6 * math.exp(-0.3)
MASKED = -1.0e30
REV = 384


class Core:

    def __init__(self, nc, ctx):
        self.nc, self.ctx, self.sems = nc, ctx, []
        self.passed = {e.engine: nc.alloc_semaphore(name=f"passed_{i}")
                       for i, e in enumerate((nc.vector, nc.tensor, nc.sync))}

    def sem(self, name):
        self.sems.append(self.nc.alloc_semaphore(name=name))
        return self.sems[-1]

    def begin(self):
        nc = self.nc
        engines = (nc.sync, nc.scalar, nc.vector, nc.tensor, nc.gpsimd)
        for i, sem in enumerate(self.sems):
            engines[i % len(engines)].sem_inc(sem, 1)
        nc.all_engine_barrier()

    def end_phase(self):
        self.nc.clear_and_free_semaphores(self.sems)
        self.nc.all_engine_barrier()
        self.sems = []


def after(count):
    return count + 1


def stand_alone(eng, core):
    eng.sem_inc(core.passed[eng.engine], 1)


def broadcast_row(ap, n):
    return ap.rearrange("(a n) -> a n", a=1).broadcast_to([P, n])


EXP_LN_SET = 6


def load_tables(nc, act, table_set):
    act.add_instruction(mybir.InstLoadActFuncSet(name=nc.get_next_instruction_name(), act_func_set_id=table_set,
                                                 engine=act.engine, ins=[], outs=[]))


def project(core, tag, x, w, groups):
    nc = core.nc
    G = len(groups)
    width = [g[1] for g in groups]
    off = [sum(width[:g]) for g in range(G)]
    W = sum(width)
    with ExitStack() as mem:
        def sb(name, shape, dt=F32):
            return mem.enter_context(nc.sbuf_tensor(f"{tag}_{name}", shape, dt))

        def ps(name):
            return mem.enter_context(nc.psum_tensor(f"{tag}_{name}", [P, BANK], F32))

        HALF = KD // 2
        STAGES = 4
        pieces = [(g, half * HALF) for g in range(G) for half in range(2)]
        stage = [sb(f"stage{i}", [P, HALF, BANK]) for i in range(STAGES)]

        def loads_to(i):
            return sum(len(groups[pieces[n][0]][0]) for n in range(i % STAGES, i + 1, STAGES))

        w_hi = sb("w_hi", [P, KD, W], F32R)
        w_lo = sb("w_lo", [P, KD, W], F32R)
        xt = [sb(f"x{i}", [P, D]) for i in range(2)]
        x_hi = [sb(f"x_hi{i}", [P, KD, P], F32R) for i in range(2)]
        x_lo = [sb(f"x_lo{i}", [P, KD, P], F32R) for i in range(2)]
        out = [sb(f"out{g}", [P, width[g]]) for g in range(G)]
        silu = [g for g in range(G) if groups[g][2] == "silu"]
        extra = {g: sb(f"extra{g}", [P, width[g]]) for g in silu}
        tanh = {g: sb(f"tanh{g}", [P, width[g]]) for g in silu}
        ps_t = [ps(f"ps_t{i}") for i in range(2)]
        ps_y = [ps(f"ps_y{g}") for g in range(G)]

        w_in = [core.sem(f"{tag}_w_in{i}") for i in range(STAGES)]
        w_hi_done = core.sem(f"{tag}_w_hi_done")
        w_lo_done = core.sem(f"{tag}_w_lo_done")
        extra_in = core.sem(f"{tag}_extra_in")
        extra_scaled = core.sem(f"{tag}_extra_scaled")
        x_in = [core.sem(f"{tag}_x_in{i}") for i in range(2)]
        xt_ready = core.sem(f"{tag}_xt_ready")
        hi_done = core.sem(f"{tag}_hi_done")
        lo_done = core.sem(f"{tag}_lo_done")
        tile_done = core.sem(f"{tag}_tile_done")
        y_ready = [core.sem(f"{tag}_y_ready{g}") for g in range(G)]
        tanh_done = {g: core.sem(f"{tag}_tanh_done{g}") for g in silu}
        chain = core.sem(f"{tag}_chain")
        out_done = [core.sem(f"{tag}_out_done{g}") for g in range(G)]
        stored = [core.sem(f"{tag}_stored{g}") for g in range(G)]

        core.begin()
        with nc.Block() as block:

            @block.sync
            def _(sp):
                def load_x(t, u):
                    sp.dma_start(xt[u][:, :], x[bass.ts(t, P), :]).then_inc(x_in[u], 16)

                load_x(0, 0)
                for i, (g, k) in enumerate(pieces):
                    if i >= STAGES:
                        sp.wait_ge(w_lo_done, after(i - STAGES + 1))
                    at = 0
                    for first, last in groups[g][0]:
                        sp.dma_start(stage[i % STAGES][:, :, at:at + last - first],
                                     w[k * P:(k + HALF) * P, first:last]
                                     .rearrange("(k p) n -> p k n", p=P)).then_inc(w_in[i % STAGES], 16)
                        at += last - first
                    if i == STAGES - 1:
                        load_x(1, 1)
                for g in silu:
                    sp.dma_start(extra[g][:, :], groups[g][4]).then_inc(extra_in, 16)

                def stores(t, nxt, u):
                    if nxt is not None:
                        sp.wait_ge(xt_ready, after(t + 1))
                        load_x(nxt, u)
                    for g in range(G):
                        sp.wait_ge(out_done[g], after(t + 1))
                        dst = groups[g][3]
                        sp.dma_start(dst[bass.ts(t, P), :], out[g][:, :]).then_inc(stored[g], 16)

                with sp.Fori(0, TILES // 2 - 1) as j:
                    for u in range(2):
                        stores(2 * j + u, 2 * j + u + 2, u)
                stores(TILES - 3, TILES - 1, 0)
                stores(TILES - 2, None, 1)
                stores(TILES - 1, None, 0)
                for g in range(G):
                    sp.wait_ge(stored[g], after(16 * TILES))

            @block.tensor
            def _(pe):
                def transposes(t, u, j):
                    pe.wait_ge(x_in[u], after(16 * j + 16))
                    pe.wait_ge(hi_done, after(t))
                    pe.wait_ge(lo_done, after(t))
                    for k in range(KD):
                        mm = nc.tensor.transpose(ps_t[k // 4][:, (k % 4) * P:(k % 4 + 1) * P],
                                                 xt[u][:, k * P:(k + 1) * P], core.ident[:, :])
                    mm.then_inc(xt_ready, 1)

                def products(t, u, after_first):
                    pe.wait_ge(hi_done, after(t + 1))
                    pe.wait_ge(lo_done, after(t + 1))
                    for g in range(G):
                        if g == 1 and after_first:
                            after_first()
                        pe.wait_ge(out_done[g], after(t))
                        cols = slice(off[g], off[g] + width[g])
                        for k in range(KD):
                            if (g, k) in pieces:
                                pe.wait_ge(w_hi_done, after(pieces.index((g, k)) + 1))
                                pe.wait_ge(w_lo_done, after(pieces.index((g, k)) + 1))
                            nc.tensor.matmul(ps_y[g][:, 0:width[g]], x_hi[u][:, k, :],
                                             w_hi[:, k, cols], start=(k == 0), stop=False)
                            nc.tensor.matmul(ps_y[g][:, 0:width[g]], x_hi[u][:, k, :],
                                             w_lo[:, k, cols], start=False, stop=False)
                            mm = nc.tensor.matmul(ps_y[g][:, 0:width[g]], x_lo[u][:, k, :],
                                                  w_hi[:, k, cols], start=False, stop=(k == KD - 1))
                        mm.then_inc(y_ready[g], 1)

                transposes(0, 0, 0)
                with pe.Fori(0, TILES // 2) as j:
                    products(2 * j, 0, lambda: transposes(2 * j + 1, 1, j))
                    products(2 * j + 1, 1, lambda: transposes(2 * j + 2, 0, j + 1))
                products(TILES - 1, 0, None)

            def high(act, t, u, first):
                act.wait_ge(xt_ready, after(t + 1))
                if not first:
                    act.wait_ge(y_ready[G - 1], after(t - 1))
                for half in range(2):
                    ins = nc.scalar.activation(x_hi[u][:, 4 * half:4 * half + 4, :], ps_t[half][:, :], ACT.Copy)
                ins.then_inc(hi_done, 1)

            @block.scalar
            def _(act):
                high(act, 0, 0, True)
                for i, (g, k) in enumerate(pieces):
                    act.wait_ge(w_in[i % STAGES], after(16 * loads_to(i)))
                    nc.scalar.activation(w_hi[:, k:k + HALF, off[g]:off[g] + width[g]],
                                         stage[i % STAGES][:, :, 0:width[g]], ACT.Copy).then_inc(w_hi_done, 1)

                def tile(t, u, more, first):
                    for g in range(G):
                        if g == 1 and more:
                            high(act, t + 1, 1 - u, first)
                        if g in silu:
                            act.wait_ge(y_ready[g], after(t + 1))
                            act.wait_ge(out_done[g], after(t))
                            nc.scalar.activation(tanh[g][:, :], ps_y[g][:, :], ACT.Tanh,
                                                 scale=0.5).then_inc(tanh_done[g], 1)
                        elif g % 2 == 0:
                            act.wait_ge(y_ready[g], after(t + 1))
                            act.wait_ge(stored[g], after(16 * t))
                            nc.scalar.activation(out[g][:, :], ps_y[g][:, 0:width[g]],
                                                 ACT.Copy).then_inc(out_done[g], 1)

                tile(0, 0, True, True)
                with act.Fori(0, TILES // 2 - 1) as j:
                    tile(2 * j + 1, 1, True, False)
                    tile(2 * j + 2, 0, True, False)
                tile(TILES - 2, 1, True, False)
                tile(TILES - 1, 0, False, False)

            @block.vector
            def _(dve):
                def low(t, u, first):
                    dve.wait_ge(hi_done, after(t + 1))
                    if not first:
                        dve.wait_ge(y_ready[G - 1], after(t - 1))
                    for half in range(2):
                        ins = nc.vector.tensor_tensor(x_lo[u][:, 4 * half:4 * half + 4, :],
                                                      ps_t[half][:, :].rearrange("p (k n) -> p k n", k=4),
                                                      x_hi[u][:, 4 * half:4 * half + 4, :].bitcast(F32),
                                                      ALU.subtract)
                    ins.then_inc(lo_done, 1)

                low(0, 0, True)
                for i, (g, k) in enumerate(pieces):
                    dve.wait_ge(w_in[i % STAGES], after(16 * loads_to(i)))
                    dve.wait_ge(w_hi_done, after(i + 1))
                    nc.vector.tensor_tensor(w_lo[:, k:k + HALF, off[g]:off[g] + width[g]],
                                            stage[i % STAGES][:, :, 0:width[g]],
                                            w_hi[:, k:k + HALF, off[g]:off[g] + width[g]].bitcast(F32),
                                            ALU.subtract).then_inc(w_lo_done, 1)
                if silu:
                    dve.wait_ge(extra_in, after(16 * len(silu)))
                    for g in silu:
                        nc.vector.tensor_scalar(extra[g][:, :], extra[g][:, :], 0.5 * groups[g][5], None,
                                                ALU.mult).then_inc(extra_scaled, 1)
                    dve.wait_ge(extra_scaled, after(len(silu)))

                def tile(t, u, more, first):
                    for g in range(G):
                        if g == 1 and more:
                            low(t + 1, 1 - u, first)
                        if g in silu:
                            dve.wait_ge(tanh_done[g], after(t + 1))
                            nc.vector.scalar_tensor_tensor(tanh[g][:, :], tanh[g][:, :], 1.0, ps_y[g][:, :],
                                                           ALU.add, ALU.mult).then_inc(chain, 1)
                            dve.wait_ge(chain, after(len(silu) * t + silu.index(g) + 1))
                            dve.wait_ge(stored[g], after(16 * t))
                            nc.vector.tensor_tensor(out[g][:, :], tanh[g][:, :], extra[g][:, :],
                                                    ALU.mult).then_inc(out_done[g], 1)
                        elif g % 2 == 1:
                            dve.wait_ge(y_ready[g], after(t + 1))
                            dve.wait_ge(stored[g], after(16 * t))
                            nc.vector.tensor_copy(out[g][:, :], ps_y[g][:, 0:width[g]]).then_inc(out_done[g], 1)

                tile(0, 0, True, True)
                with dve.Fori(0, TILES // 2 - 1) as j:
                    tile(2 * j + 1, 1, True, False)
                    tile(2 * j + 2, 0, True, False)
                tile(TILES - 2, 1, True, False)
                tile(TILES - 1, 0, False, False)


def recurrence(core, qka, v, w_a2, b_a, o, state0, state_prompt, state_sample):
    nc = core.nc
    QKA = 2 * GK + G_LOW
    with ExitStack() as mem:
        def sb(name, shape, dt=F32):
            return mem.enter_context(nc.sbuf_tensor(f"gla_{name}", shape, dt))

        def ps(name, n=BANK):
            return mem.enter_context(nc.psum_tensor(f"gla_{name}", [P, n], F32))

        KINDS = {"p": G_CHUNK, "s": DEC_SEQ}
        SPANS = {"p": P, "s": DEC_SEQ}
        SUMS = [(), (0,), (0, 1), (0, 1, 2), (0,), (2,), (0, 1), (1,), (), (2,), (0, 1, 2, 3)]
        FROM_START, TO_CHUNK_END, TO_MIDDLE, FROM_MIDDLE, WHOLE = 0, 4, 6, 8, 10
        NS = {"p": len(SUMS), "s": P // DEC_SEQ}
        HALF = P // 2
        m_cum = {c: sb(f"m_cum_{c}", [P, P]) for c in KINDS}
        m_rem = {c: sb(f"m_rem_{c}", [P, P]) for c in KINDS}
        m_tot = {c: sb(f"m_tot_{c}", [P, NS[c]]) for c in KINDS}
        m_att = {c: sb(f"m_att_{c}", [P, P], I32) for c in KINDS}
        row_of = sb("row_of", [P, P // DEC_SEQ])
        w2 = sb("w2", [G_LOW, GK])
        ba = sb("ba", [P, GK])
        x = [sb(f"x{i}", [P, QKA]) for i in range(2)]
        vt = [sb(f"v{i}", [P, GV]) for i in range(2)]
        a_t = sb("a_t", [G_LOW, P])
        z = sb("z", [P, GK])
        za = sb("za", [P, GK])
        la = sb("la", [P, GK])
        e_cum = sb("e_cum", [P, GK])
        e_inv = sb("e_inv", [P, GK])
        e_rem = sb("e_rem", [P, GK])
        e_tot = [sb(f"e_tot{i}", [P, G_HEADS * P // DEC_SEQ]) for i in range(2)]
        q_dec = sb("q_dec", [P, GK])
        k_inv = sb("k_inv", [P, GK])
        k_end = [sb(f"k_end{i}", [P, GK]) for i in range(2)]
        q_t = sb("q_t", [P, GK])
        k_t = sb("k_t", [P, GK])
        q_start = [sb(f"q_start{i}", [P, GK]) for i in range(2)]
        k_chunk = sb("k_chunk", [P, G_HEADS, 2, G_CHUNK])
        k_mid = sb("k_mid", [P, G_HEADS, HALF])
        q_mid = sb("q_mid", [P, G_HEADS, HALF])
        att = [sb(f"att{i}", [P, G_HEADS, P]) for i in range(2)]
        S = [sb(f"S{i}", [P, GV]) for i in range(2)]
        out = [sb(f"out{i}", [P, GV]) for i in range(2)]
        q_one = sb("q_one", [P, DEC_BATCH, G_HEADS, SAMPLE_ROWS])
        k_one = [sb(f"k_one{i}", [P, GK]) for i in range(2)]
        STATES = 4
        s_in = [sb(f"s_in{i}", [P, GV]) for i in range(STATES)]
        s_out = [sb(f"s_out{i}", [P, GV]) for i in range(2)]
        ps_z, ps_cum, ps_rem, ps_small = ps("ps_z"), ps("ps_cum"), ps("ps_rem"), ps("ps_small")
        ps_o, ps_kv = ps("ps_o", GV), ps("ps_kv", GV)

        names = ("masks weights_in stored_state a_ready a_copied z_ready z_added z_abs z_exp z_ln la_done "
                 "cum_ready rem_ready cum_exp rem_exp q_done k_done kend_done t_ready qt_done kt_done scaled qs_done "
                 "att_ready att_done "
                 "o_ready o_half0 o_half1 kv_ready s_done "
                 "q_split k_split out_in s_init").split()
        s = {n: core.sem(f"gla_{n}") for n in names}
        x_in = [core.sem(f"gla_x_in{i}") for i in range(2)]
        v_in = [core.sem(f"gla_v_in{i}") for i in range(2)]
        stored = [core.sem(f"gla_stored{i}") for i in range(2)]
        st_in = [core.sem(f"gla_state_in{i}") for i in range(STATES)]
        st_out = [core.sem(f"gla_state_out{i}") for i in range(2)]

        def by_chunk(ap):
            return ap.rearrange("p (h c n) -> p h c n", h=G_HEADS, n=G_CHUNK)

        def factor(u, first, n):
            return (e_tot[u][:, 0:G_HEADS * NS["p"]].rearrange("p (h n) -> p h n", h=G_HEADS)
                    [:, :, first:first + n].unsqueeze(3).broadcast_to([P, G_HEADS, n, G_CHUNK]))

        def kv_of(b, h):
            if b % 2 == 0:
                return ps_kv[:, h * G_DV:(h + 1) * G_DV]
            return (ps_cum, ps_rem)[h // 2][:, (h % 2) * G_DV:(h % 2 + 1) * G_DV]

        core.begin()
        with nc.Block() as block:

            def store_state(sp, b):
                sp.wait_ge(s["s_done"], after(PROMPT_TILES + b + 1))
                sp.dma_start(state_sample[b].rearrange("h k v -> k h v"),
                             s_out[b % 2][:, :].rearrange("p (h v) -> p h v", h=G_HEADS)).then_inc(st_out[b % 2], 16)

            @block.sync
            def _(sp):
                sp.dma_start(w2[:, :], w_a2).then_inc(s["weights_in"], 16)
                sp.dma_start(ba[:, :], broadcast_row(b_a, GK)).then_inc(s["weights_in"], 16)

                def load_x(t, u):
                    sp.dma_start(x[u][:, :], qka[bass.ts(t, P), :]).then_inc(x_in[u], 16)

                def load_v(t, u):
                    sp.dma_start(vt[u][:, :], v[bass.ts(t, P), :]).then_inc(v_in[u], 16)

                def next_x(t, u):
                    sp.wait_ge(s["q_done"], after(t - 1))
                    stand_alone(sp, core)
                    sp.wait_ge(s["k_done"], after(t - 1))
                    stand_alone(sp, core)
                    sp.wait_ge(s["kend_done"], after(t - 1))
                    stand_alone(sp, core)
                    load_x(t, u)

                def next_v(t, u):
                    sp.wait_ge(s["kv_ready"], after(t - 1))
                    stand_alone(sp, core)
                    load_v(t, u)

                def store(t, u):
                    sp.wait_ge(s["o_half0"], after(t + 1))
                    sp.wait_ge(s["o_half1"], after(t + 1))
                    sp.dma_start(o[bass.ts(t, P), :], out[u][:, :]).then_inc(stored[u], 16)

                def step(t, u):
                    next_x(t + 3, 1 - u)
                    next_v(t + 2, u)
                    store(t, u)

                def load_state(b):
                    sp.dma_start(s_in[b % STATES][:, :].rearrange("p (h v) -> p h v", h=G_HEADS),
                                 state0[b].rearrange("h k v -> k h v")).then_inc(st_in[b % STATES], 16)

                for i in range(2):
                    load_x(i, i)
                    load_v(i, i)
                for b in range(STATES):
                    load_state(b)
                next_x(2, 0)
                with sp.Fori(0, PROMPT_TILES // 2 - 1) as j:
                    step(2 * j, 0)
                    step(2 * j + 1, 1)
                next_v(PROMPT_TILES, 0)
                store(PROMPT_TILES - 2, 0)
                store(PROMPT_TILES - 1, 1)
                sp.wait_ge(s["s_done"], after(PROMPT_TILES))
                sp.dma_start(state_prompt.rearrange("h k v -> k h v"),
                             S[0][:, :].rearrange("p (h v) -> p h v", h=G_HEADS)).then_inc(s["stored_state"], 16)
                for b in range(DEC_BATCH):
                    store_state(sp, b)
                    if b + STATES < DEC_BATCH:
                        load_state(b + STATES)
                store(PROMPT_TILES, 0)
                sp.wait_ge(s["stored_state"], after(16))
                for u in range(2):
                    sp.wait_ge(st_out[u], after(16 * (DEC_BATCH // 2)))
                sp.wait_ge(stored[0], after(16 * (PROMPT_TILES // 2 + 1)))
                sp.wait_ge(stored[1], after(16 * (PROMPT_TILES // 2)))

            @block.gpsimd
            def _(pool):
                count = [0]

                def select(ap, op, fill, base, pattern, mult):
                    pool.wait_ge(s["masks"], after(count[0]))
                    nc.gpsimd.affine_select(out=ap, in_=ap, compare_op=op, fill=fill, base=base,
                                            pattern=pattern, channel_multiplier=mult).then_inc(s["masks"], 1)
                    count[0] += 1

                def fill(ap, value):
                    pool.wait_ge(s["masks"], after(count[0]))
                    nc.gpsimd.memset(ap, value).then_inc(s["masks"], 1)
                    count[0] += 1

                def within(m, n):
                    nb = P // n
                    view = m[:, :].rearrange("p (b n) -> p b n", b=nb)
                    select(view, ALU.is_ge, 0.0, 0, [[-n, nb], [0, n]], 1)
                    select(view, ALU.is_ge, 0.0, n - 1, [[n, nb], [0, n]], -1)

                for c, n in KINDS.items():
                    for m, unit, span in ((m_cum[c], 1 / G_TAU, n), (m_att[c], 1, SPANS[c])):
                        fill(m[:, :], unit)
                        if span < P:
                            within(m, span)
                        select(m[:, :], ALU.is_ge, 0.0, 0, [[1, P]], -1)
                    fill(m_rem[c][:, :], 1 / G_TAU)
                    if SPANS[c] < P:
                        within(m_rem[c], SPANS[c])
                    select(m_rem[c][:, :], ALU.is_gt, 0.0, 0, [[-1, P]], 1)
                fill(m_tot["p"][:, :], 0.0)
                for j, chunks in enumerate(SUMS):
                    if chunks:
                        fill(m_tot["p"][chunks[0] * G_CHUNK:(chunks[-1] + 1) * G_CHUNK, j:j + 1], 1 / G_TAU)
                for m, unit in ((m_tot["s"], 1 / G_TAU), (row_of, 1.0)):
                    n, nb = DEC_SEQ, P // DEC_SEQ
                    fill(m[:, :], unit)
                    select(m[:, :], ALU.is_ge, 0.0, 0, [[-n, nb]], 1)
                    select(m[:, :], ALU.is_ge, 0.0, n - 1, [[n, nb]], -1)
                for i in range(2):
                    fill(att[i][:, :, :], 0.0)
                fill(S[0][:, :], 0.0)
                fill(q_one[:, :, :, :], 0.0)
                core.gla_masks = count[0]

                def ends(t, u, first):
                    pool.wait_ge(s["rem_exp"], after(t + 1))
                    if not first:
                        pool.wait_ge(s["kv_ready"], after(t - 1))
                    nc.gpsimd.tensor_tensor(k_end[u][:, :], x[u][:, GK:2 * GK], e_rem[:, :],
                                            ALU.mult).then_inc(s["kend_done"], 1)

                def starts(t, u):
                    pool.wait_ge(s["qt_done"], after(t + 1))
                    nc.gpsimd.tensor_tensor(by_chunk(q_start[u][:, :]), by_chunk(q_t[:, :]),
                                            factor(u, FROM_START, CHUNKS), ALU.mult).then_inc(s["qs_done"], 1)

                for i in range(2):
                    ends(i, i, True)
                    starts(i, i)
                with pool.Fori(1, PROMPT_TILES // 2) as j:
                    for i in range(2):
                        ends(2 * j + i, i, False)
                        starts(2 * j + i, i)
                ends(TILES - 1, 0, False)

            masks = core.gla_masks

            @block.tensor
            def _(pe):
                def low_rank(t, u, j):
                    pe.wait_ge(x_in[u], after(16 * j + 16))
                    if not (isinstance(t, int) and t < 2):
                        pe.wait_ge(s["rem_exp"], after(t - 1))
                    nc.tensor.transpose(ps_small[0:G_LOW, 0:P], x[u][:, 2 * GK:QKA],
                                        core.ident[:, :]).then_inc(s["a_ready"], 1)

                def decay_logits(t):
                    pe.wait_ge(s["a_copied"], after(t + 1))
                    if not (isinstance(t, int) and t < 2):
                        pe.wait_ge(s["att_done"], after(t - 1))
                    nc.tensor.matmul(ps_z[:, :], a_t[:, :], w2[:, :], start=True, stop=True).then_inc(s["z_ready"], 1)

                def sums(t, c):
                    pe.wait_ge(s["la_done"], after(t + 1))
                    pe.wait_ge(s["qt_done"], after(t))
                    pe.wait_ge(s["kt_done"], after(t))
                    nc.tensor.matmul(ps_cum[:, :], m_cum[c][:, :], la[:, :], start=True,
                                     stop=True).then_inc(s["cum_ready"], 1)
                    nc.tensor.matmul(ps_rem[:, :], m_rem[c][:, :], la[:, :], start=True, stop=True)
                    if c == "p":
                        pe.wait_ge(s["a_copied"], after(t + 2))
                    n = NS[c]
                    for h in range(G_HEADS):
                        mm = nc.tensor.matmul(ps_small[:, P + h * n:P + (h + 1) * n],
                                              la[:, h * G_DK:(h + 1) * G_DK], m_tot[c][:, :],
                                              start=True, stop=True)
                    mm.then_inc(s["rem_ready"], 1)

                def turn(t):
                    pe.wait_ge(s["q_done"], after(t + 1))
                    pe.wait_ge(s["k_done"], after(t + 1))
                    pe.wait_ge(s["rem_exp"], after(t + 1))
                    for src, dst in ((q_dec, ps_cum), (k_inv, ps_rem)):
                        for h in range(G_HEADS):
                            mm = nc.tensor.transpose(dst[:, h * P:(h + 1) * P], src[:, h * P:(h + 1) * P],
                                                     core.ident[:, :])
                    mm.then_inc(s["t_ready"], 1)

                def scores(t, c):
                    pe.wait_ge(s["qt_done"], after(t + 1))
                    pe.wait_ge(s["kt_done"], after(t + 1))
                    if c == "p":
                        pe.wait_ge(s["scaled"], after(t + 1))
                        pe.wait_ge(s["z_added"], after(t + 2))
                    for h in range(G_HEADS):
                        at = h * P
                        mm = nc.tensor.matmul(ps_z[:, at:at + P], k_t[:, at:at + P], q_t[:, at:at + P],
                                              start=True, stop=True, skip_group_check=True)
                        if c == "p":
                            for i in range(2):
                                first, second = 2 * i * G_CHUNK, (2 * i + 1) * G_CHUNK
                                nc.tensor.matmul(ps_z[first:second, at + second:at + second + G_CHUNK],
                                                 k_chunk[:, h, i, :], q_t[:, at + second:at + second + G_CHUNK],
                                                 start=True, stop=True, skip_group_check=True)
                            mm = nc.tensor.matmul(ps_z[0:HALF, at + HALF:at + P], k_mid[:, h, :], q_mid[:, h, :],
                                                  start=True, stop=True, skip_group_check=True)
                    mm.then_inc(s["att_ready"], 1)

                def intra(t, u, j):
                    pe.wait_ge(s["att_done"], after(t + 1))
                    pe.wait_ge(v_in[u], after(16 * j + 16))
                    pe.wait_ge(s["o_half0"], after(t))
                    pe.wait_ge(s["o_half1"], after(t))
                    for h in range(G_HEADS):
                        nc.tensor.matmul(ps_o[:, h * G_DV:(h + 1) * G_DV], att[u][:, h, :],
                                         vt[u][:, h * G_DV:(h + 1) * G_DV], start=(h % 2 == 0), stop=False,
                                         skip_group_check=True)

                def state(t, u):
                    pe.wait_ge(s["qs_done"], after(t + 1))
                    pe.wait_ge(s["s_done"], after(t))
                    for h in range(G_HEADS):
                        mm = nc.tensor.matmul(ps_o[:, h * G_DV:(h + 1) * G_DV], q_start[u][:, h * P:(h + 1) * P],
                                              S[u][:, h * G_DV:(h + 1) * G_DV], start=False, stop=True,
                                              skip_group_check=True)
                    mm.then_inc(s["o_ready"], 1)
                    pe.wait_ge(s["kend_done"], after(t + 1))
                    for h in range(G_HEADS):
                        mm = nc.tensor.matmul(ps_kv[:, h * G_DV:(h + 1) * G_DV], k_end[u][:, h * P:(h + 1) * P],
                                              vt[u][:, h * G_DV:(h + 1) * G_DV], start=True, stop=True,
                                              skip_group_check=True)
                    mm.then_inc(s["kv_ready"], 1)

                def tile(t, u, j, c, more=True):
                    if more:
                        low_rank(t + 2, u, j + 1)
                    sums(t + 1, c)
                    if more:
                        decay_logits(t + 2)
                    intra(t, u, j)
                    turn(t + 1)
                    state(t, u)
                    scores(t + 1, c)

                pe.wait_ge(s["weights_in"], after(32))
                low_rank(0, 0, 0)
                decay_logits(0)
                low_rank(1, 1, 0)
                pe.wait_ge(s["masks"], after(masks))
                sums(0, "p")
                pe.wait_ge(s["z_added"], after(1))
                decay_logits(1)
                turn(0)
                scores(0, "p")
                with pe.Fori(0, PROMPT_TILES // 2 - 1) as j:
                    tile(2 * j, 0, j, "p")
                    tile(2 * j + 1, 1, j, "p")
                last = PROMPT_TILES // 2 - 1
                tile(PROMPT_TILES - 2, 0, last, "p")
                tile(PROMPT_TILES - 1, 1, last, "s", False)
                intra(PROMPT_TILES, 0, last + 1)
                pe.wait_ge(s["q_split"], after(1))
                R = SAMPLE_ROWS
                for b in range(DEC_BATCH):
                    pe.wait_ge(s["k_split"], after(b + 1))
                    pe.wait_ge(s["s_done"], after(PROMPT_TILES + max(b - 1, 0)))
                    for h in range(G_HEADS):
                        mm = nc.tensor.matmul(kv_of(b, h),
                                              k_one[b % 2][:, h * P:(h + 1) * P],
                                              vt[0][:, h * G_DV:(h + 1) * G_DV], start=True, stop=True,
                                              skip_group_check=True)
                    mm.then_inc(s["kv_ready"], 1)
                    pe.wait_ge(st_in[b % STATES], after(16 * (b // STATES + 1)))
                    for h in range(G_HEADS):
                        mm = nc.tensor.matmul(ps_o[0:R, h * G_DV:(h + 1) * G_DV], q_one[:, b, h, :],
                                              s_in[b % STATES][:, h * G_DV:(h + 1) * G_DV], start=False, stop=True,
                                              skip_group_check=True)
                    mm.then_inc(s["out_in"], 1)
                    if b == DEC_BATCH - 1:
                        mm = nc.tensor.matmul(ps_small[0:1, 0:1], core.ident[:, 0:1], core.ident[:, 0:1],
                                              start=True, stop=True)
                        mm.then_inc(s["o_ready"], 1)

            @block.scalar
            def _(act):
                def low_rank(t):
                    act.wait_ge(s["a_ready"], after(t + 1))
                    nc.scalar.activation(a_t[:, :], ps_small[0:G_LOW, 0:P], ACT.Copy).then_inc(s["a_copied"], 1)

                def softplus(t):
                    act.wait_ge(s["z_added"], after(t + 1))
                    nc.scalar.activation(za[:, :], z[:, :], ACT.Abs).then_inc(s["z_abs"], 1)
                    act.wait_ge(s["z_abs"], after(t + 1))
                    nc.scalar.activation(za[:, :], za[:, :], ACT.Exp, scale=-1.0).then_inc(s["z_exp"], 1)
                    act.wait_ge(s["z_exp"], after(t + 1))
                    nc.scalar.activation(za[:, :], za[:, :], ACT.Ln, bias=1.0).then_inc(s["z_ln"], 1)

                def exps(t, u, c):
                    act.wait_ge(s["cum_ready"], after(t + 1))
                    act.wait_ge(s["q_done"], after(t))
                    act.wait_ge(s["k_done"], after(t))
                    nc.scalar.activation(e_cum[:, :], ps_cum[:, :], ACT.Exp)
                    nc.scalar.activation(e_inv[:, :], ps_cum[:, :], ACT.Exp, scale=-1.0).then_inc(s["cum_exp"], 1)
                    act.wait_ge(s["rem_ready"], after(t + 1))
                    if not (isinstance(t, int) and t < 2):
                        act.wait_ge(s["s_done"], after(t - 1))
                        act.wait_ge(s["qs_done"], after(t - 1))
                        act.wait_ge(s["scaled"], after(t - 1))
                    n = G_HEADS * NS[c]
                    nc.scalar.activation(e_tot[u][:, 0:n], ps_small[:, P:P + n], ACT.Exp)
                    act.wait_ge(s["kend_done"], after(t))
                    nc.scalar.activation(e_rem[:, :], ps_rem[:, :], ACT.Exp).then_inc(s["rem_exp"], 1)

                def queries(t):
                    act.wait_ge(s["t_ready"], after(t + 1))
                    act.wait_ge(s["att_ready"], after(t))
                    act.wait_ge(s["qs_done"], after(t))
                    act.wait_ge(s["scaled"], after(t))
                    nc.scalar.activation(q_t[:, :], ps_cum[:, :], ACT.Copy).then_inc(s["qt_done"], 1)

                def back(t, u, j):
                    act.wait_ge(s["o_ready"], after(t + 1))
                    act.wait_ge(stored[u], after(16 * j))
                    nc.scalar.activation(out[u][:, 0:BANK], ps_o[:, 0:BANK], ACT.Copy).then_inc(s["o_half0"], 1)

                def tile(t, u, j, c, more=True):
                    if more:
                        low_rank(t + 2)
                    exps(t + 1, 1 - u, c)
                    if more:
                        softplus(t + 2)
                    queries(t + 1)
                    back(t, u, j)

                load_tables(nc, act, EXP_LN_SET)
                low_rank(0)
                softplus(0)
                low_rank(1)
                exps(0, 0, "p")
                softplus(1)
                queries(0)
                with act.Fori(0, PROMPT_TILES // 2 - 1) as j:
                    tile(2 * j, 0, j, "p")
                    tile(2 * j + 1, 1, j, "p")
                last = PROMPT_TILES // 2 - 1
                tile(PROMPT_TILES - 2, 0, last, "p")
                tile(PROMPT_TILES - 1, 1, last, "s", False)
                back(PROMPT_TILES, 0, last + 1)

            @block.vector
            def _(dve):
                def add_bias(t):
                    dve.wait_ge(s["z_ready"], after(t + 1))
                    nc.vector.tensor_tensor(z[:, :], ps_z[:, :], ba[:, :], ALU.add).then_inc(s["z_added"], 1)

                def log_decay(t):
                    dve.wait_ge(s["z_ln"], after(t + 1))
                    dve.wait_ge(s["rem_ready"], after(t))
                    nc.vector.scalar_tensor_tensor(la[:, :], z[:, :], 0.0, za[:, :], ALU.min,
                                                   ALU.subtract).then_inc(s["la_done"], 1)

                def decayed(t, u):
                    dve.wait_ge(s["cum_exp"], after(t + 1))
                    dve.wait_ge(s["t_ready"], after(t))
                    nc.vector.scalar_tensor_tensor(q_dec[:, :], x[u][:, 0:GK], G_DK ** -0.5, e_cum[:, :],
                                                   ALU.mult, ALU.mult).then_inc(s["q_done"], 1)
                    nc.vector.tensor_tensor(k_inv[:, :], x[u][:, GK:2 * GK], e_inv[:, :],
                                            ALU.mult).then_inc(s["k_done"], 1)

                def keys(t, u, c):
                    dve.wait_ge(s["t_ready"], after(t + 1))
                    dve.wait_ge(s["att_ready"], after(t))
                    turned = by_chunk(ps_rem[:, :])
                    if c == "p":
                        stand_alone(dve, core)
                        nc.vector.tensor_tensor(k_mid[:, :, :].rearrange("p h (c n) -> p h c n", n=G_CHUNK),
                                                turned[:, :, 0:2, :], factor(u, TO_MIDDLE, 2), ALU.mult)
                        nc.vector.tensor_tensor(k_chunk[:, :, :, :], turned[:, :, 0::2, :],
                                                factor(u, TO_CHUNK_END, 2), ALU.mult)
                    nc.vector.tensor_copy(k_t[:, :], ps_rem[:, :]).then_inc(s["kt_done"], 1)
                    if c == "p":
                        dve.wait_ge(s["qt_done"], after(t + 1))
                        nc.vector.tensor_tensor(q_mid[:, :, :].rearrange("p h (c n) -> p h c n", n=G_CHUNK),
                                                by_chunk(q_t[:, :])[:, :, 2:4, :], factor(u, FROM_MIDDLE, 2),
                                                ALU.mult).then_inc(s["scaled"], 1)

                def causal(t, u, c):
                    dve.wait_ge(s["att_ready"], after(t + 1))
                    stand_alone(dve, core)
                    for h in range(G_HEADS):
                        ins = nc.vector.copy_predicated(att[u][:, h, :], m_att[c][:, :],
                                                        ps_z[:, h * P:(h + 1) * P])
                    ins.then_inc(s["att_done"], 1)

                def update(t, u):
                    dve.wait_ge(s["kv_ready"], after(t + 1))
                    dve.wait_ge(s["s_done"], after(t))
                    for h in range(G_HEADS):
                        cols = slice(h * G_DV, (h + 1) * G_DV)
                        whole = h * NS["p"] + WHOLE
                        ins = nc.vector.scalar_tensor_tensor(S[1 - u][:, cols], S[u][:, cols],
                                                             e_tot[u][:, whole:whole + 1],
                                                             ps_kv[:, cols], ALU.mult, ALU.add)
                    ins.then_inc(s["s_done"], 1)

                def back(t, u, j):
                    dve.wait_ge(s["o_ready"], after(t + 1))
                    dve.wait_ge(stored[u], after(16 * j))
                    nc.vector.tensor_copy(out[u][:, BANK:GV], ps_o[:, BANK:GV]).then_inc(s["o_half1"], 1)

                def tile(t, u, j, c, more=True):
                    if more:
                        add_bias(t + 2)
                    decayed(t + 1, 1 - u)
                    if more:
                        log_decay(t + 2)
                    keys(t + 1, 1 - u, c)
                    back(t, u, j)
                    update(t, u)
                    if c == "s":
                        nc.vector.memset(att[1 - u][:, :, :], 0.0).then_inc(s["s_init"], 1)
                        dve.wait_ge(s["s_init"], after(1))
                    causal(t + 1, 1 - u, c)

                dve.wait_ge(s["weights_in"], after(32))
                add_bias(0)
                log_decay(0)
                add_bias(1)
                decayed(0, 0)
                log_decay(1)
                keys(0, 0, "p")
                dve.wait_ge(s["masks"], after(masks))
                causal(0, 0, "p")
                with dve.Fori(0, PROMPT_TILES // 2 - 1) as j:
                    tile(2 * j, 0, j, "p")
                    tile(2 * j + 1, 1, j, "p")
                last = PROMPT_TILES // 2 - 1
                tile(PROMPT_TILES - 2, 0, last, "p")
                tile(PROMPT_TILES - 1, 1, last, "s", False)
                dve.wait_ge(s["qt_done"], after(TILES))
                for b in range(DEC_BATCH):
                    cols = slice(b * DEC_SEQ, (b + 1) * DEC_SEQ)
                    ins = nc.vector.tensor_copy(q_one[:, b, :, cols],
                                                q_t[:, :].rearrange("p (h n) -> p h n", h=G_HEADS)[:, :, cols])
                ins.then_inc(s["q_split"], 1)
                dve.wait_ge(s["kend_done"], after(TILES))
                nb = P // DEC_SEQ
                base = PROMPT_TILES

                def one_key(b):
                    nc.vector.tensor_scalar(k_one[b % 2][:, :], k_end[0][:, :], row_of[:, b:b + 1], None,
                                            ALU.mult).then_inc(s["k_split"], 1)

                one_key(0)
                for b in range(DEC_BATCH):
                    if b + 1 < DEC_BATCH:
                        if b >= 1:
                            dve.wait_ge(s["kv_ready"], after(base + b))
                        one_key(b + 1)
                    dve.wait_ge(s["kv_ready"], after(base + b + 1))
                    dve.wait_ge(s["out_in"], after(b + 1))
                    dve.wait_ge(st_in[b % STATES], after(16 * (b // STATES + 1)))
                    if b >= 2:
                        dve.wait_ge(st_out[b % 2], after(16 * (b // 2)))
                    for h in range(G_HEADS):
                        cols = slice(h * G_DV, (h + 1) * G_DV)
                        ins = nc.vector.scalar_tensor_tensor(s_out[b % 2][:, cols], s_in[b % STATES][:, cols],
                                                             e_tot[0][:, h * nb + b:h * nb + b + 1],
                                                             kv_of(b, h), ALU.mult, ALU.add)
                    ins.then_inc(s["s_done"], 1)
                back(PROMPT_TILES, 0, PROMPT_TILES // 2)


def residual(core, tag, x, o, heads, factors, p, w_out, ln_g, ln_b, w_gate, w_proj, y):
    nc = core.nc
    with ExitStack() as mem:
        def sb(name, shape, dt=F32):
            return mem.enter_context(nc.sbuf_tensor(f"{tag}_{name}", shape, dt))

        def ps(name, n=BANK):
            return mem.enter_context(nc.psum_tensor(f"{tag}_{name}", [P, n], F32))

        weights = [(w_out, KD), (w_gate, KD), (w_proj, KP)]
        loads = [(n, k) for n, (_, count) in enumerate(weights) for k in range(count)]
        loaded = [sum(count for _, count in weights[:n + 1]) for n in range(len(weights))]
        w_hi = [sb(f"w_hi{n}", [P, k, D], F32R) for n, (_, k) in enumerate(weights)]
        w_lo = [sb(f"w_lo{n}", [P, k, D], F32R) for n, (_, k) in enumerate(weights)]
        ft = sb("factors", [P, D])
        sq = sb("squares", [P, D])
        ms = sb("ms", [P, heads])
        gb = sb("ln_g", [P, D])
        bb = sb("ln_b", [P, D])
        ot = sb("o", [P, D])
        xt = sb("x", [P, D])
        pt = [sb(f"p{i}", [P, PLE]) for i in range(2)]
        hi = {"o": sb("o_hi", [P, KD, P], F32R), "p": sb("p_hi", [P, KP, P], F32R), "h": sb("h_hi", [P, KD, P], F32R)}
        lo = {"o": sb("o_lo", [P, KD, P], F32R), "p": sb("p_lo", [P, KP, P], F32R), "h": sb("h_lo", [P, KD, P], F32R)}
        stats = sb("stats", [P, 2, 6])
        mv = sb("mv", [P, 2])
        rstd = sb("rstd", [P, 1])
        h = [sb(f"h{i}", [P, D]) for i in range(2)]
        expo = sb("expo", [P, D])
        out = sb("out", [P, D])
        stage = [h[0], h[1], expo, out]
        SCALE_AT, PART_AT, NEXT_AT = 5, 9, 16
        STAGES = len(stage)
        ps_f, ps_g, ps_p, ps_t = ps("ps_f", D), ps("ps_g", D), ps("ps_p", D), ps("ps_t", D)
        bank = {"o": ps_t, "h": ps_t, "p": ps_p}
        KS = {"o": KD, "p": KP, "h": KD}

        s = {n: core.sem(f"{tag}_{n}") for n in
             ("w_hi_done w_lo_done f_in squared ms_done ms_eps rms_done o_normed o_scaled rows_in o_in x_in o_t p_t h_t o_hi o_lo p_hi p_lo h_hi h_lo "
              "f_ready g_ready p_ready y_done norm_stat norm_mv norm_eps rstd_done h_norm h_scaled h_done "
              "e_done e_mul out_done stored").split()}
        w_in = [core.sem(f"{tag}_w_in{i}") for i in range(STAGES)]
        p_in = [core.sem(f"{tag}_p_in{i}") for i in range(2)]

        core.begin()
        with nc.Block() as block:

            @block.sync
            def _(sp):
                def load_o(t):
                    sp.dma_start(ft[:, :], factors[bass.ts(t, P), :]).then_inc(s["f_in"], 16)
                    sp.dma_start(ot[:, :], o[bass.ts(t, P), :]).then_inc(s["o_in"], 16)

                def load_x(t):
                    sp.dma_start(xt[:, :], x[bass.ts(t, P), :]).then_inc(s["x_in"], 16)

                def load_p(t, u):
                    sp.dma_start(pt[u][:, :], p[bass.ts(t, P), :]).then_inc(p_in[u], 16)

                for i, (n, k) in enumerate(loads):
                    if i == 2:
                        load_o(0)
                    if i == NEXT_AT - 3:
                        sp.wait_ge(s["o_t"], after(1))
                        load_o(1)
                    if i >= STAGES:
                        sp.wait_ge(s["w_lo_done"], after(i - STAGES + 1))
                    sp.dma_start(stage[i % STAGES][:, :],
                                 weights[n][0][k * P:(k + 1) * P, :]).then_inc(w_in[i % STAGES], 16)
                sp.dma_start(gb[:, :], broadcast_row(ln_g, D)).then_inc(s["rows_in"], 16)
                sp.dma_start(bb[:, :], broadcast_row(ln_b, D)).then_inc(s["rows_in"], 16)
                load_x(0)
                load_p(0, 0)
                load_p(1, 1)
                sp.wait_ge(s["o_t"], after(2))
                load_o(2)
                sp.wait_ge(s["y_done"], after(1))
                load_x(1)

                def step(t, u, more=True, more_o=True):
                    if more:
                        sp.wait_ge(s["p_t"], after(t + 1))
                        load_p(t + 2, u)
                    if more_o:
                        sp.wait_ge(s["o_t"], after(t + 3))
                        load_o(t + 3)
                    if more:
                        sp.wait_ge(s["y_done"], after(t + 2))
                        load_x(t + 2)
                    sp.wait_ge(s["out_done"], after(t + 1))
                    sp.dma_start(y[bass.ts(t, P), :], out[:, :]).then_inc(s["stored"], 16)

                with sp.Fori(0, TILES // 2 - 1) as j:
                    step(2 * j, 0)
                    step(2 * j + 1, 1)
                step(TILES - 3, 0, more_o=False)
                step(TILES - 2, 1, more=False, more_o=False)
                step(TILES - 1, 0, more=False, more_o=False)
                sp.wait_ge(s["stored"], after(16 * TILES))

            @block.tensor
            def _(pe):
                def turn(src, dst, k_count, ready):
                    for k in range(k_count):
                        mm = nc.tensor.transpose(dst[:, k * P:(k + 1) * P], src[:, k * P:(k + 1) * P],
                                                 core.ident[:, :])
                    mm.then_inc(ready, 1)

                def product(dst, kind, n, ready):
                    K = KS[kind]
                    for half in range(2):
                        cols = slice(half * BANK, (half + 1) * BANK)
                        for k in range(K):
                            nc.tensor.matmul(dst[:, cols], hi[kind][:, k, :], w_hi[n][:, k, cols],
                                             start=(k == 0), stop=False)
                            nc.tensor.matmul(dst[:, cols], hi[kind][:, k, :], w_lo[n][:, k, cols],
                                             start=False, stop=False)
                            mm = nc.tensor.matmul(dst[:, cols], lo[kind][:, k, :], w_hi[n][:, k, cols],
                                                  start=False, stop=(k == K - 1))
                    mm.then_inc(ready, 1)

                def turn_o(t, wait_h):
                    pe.wait_ge(s["o_scaled"], after(t + 1))
                    if wait_h:
                        pe.wait_ge(s["h_hi"], after(t - 1))
                        pe.wait_ge(s["h_lo"], after(t - 1))
                    turn(ot, ps_t, KD, s["o_t"])

                def turn_h(t, u, turned_o):
                    pe.wait_ge(s["h_done"], after(t + 1))
                    pe.wait_ge(s["o_hi"], after(turned_o))
                    pe.wait_ge(s["o_lo"], after(turned_o))
                    turn(h[u], ps_t, KD, s["h_t"])

                def turn_p(t, u, j):
                    pe.wait_ge(p_in[u], after(16 * j + 16))
                    pe.wait_ge(s["e_mul"], after(t))
                    turn(pt[u], ps_p, KP, s["p_t"])

                def first(t):
                    pe.wait_ge(s["o_hi"], after(t + 1))
                    pe.wait_ge(s["o_lo"], after(t + 1))
                    pe.wait_ge(s["y_done"], after(t))
                    product(ps_f, "o", 0, s["f_ready"])

                def middle(t):
                    pe.wait_ge(s["p_hi"], after(t + 1))
                    pe.wait_ge(s["p_lo"], after(t + 1))
                    product(ps_p, "p", 2, s["p_ready"])

                def second(t):
                    pe.wait_ge(s["h_hi"], after(t + 1))
                    pe.wait_ge(s["h_lo"], after(t + 1))
                    pe.wait_ge(s["e_done"], after(t))
                    product(ps_g, "h", 1, s["g_ready"])

                def wait_weights(n):
                    pe.wait_ge(s["w_hi_done"], after(loaded[n]))
                    pe.wait_ge(s["w_lo_done"], after(loaded[n]))

                def tile(t, u, j, more=True):
                    turn_h(t, u, t + 2)
                    first(t + 1)
                    turn_p(t, u, j)
                    if more:
                        turn_o(t + 2, True)
                    second(t)
                    middle(t)

                turn_o(0, False)
                wait_weights(0)
                first(0)
                turn_o(1, False)
                wait_weights(1)
                wait_weights(2)
                last = TILES // 2 - 1
                with pe.Fori(0, last) as j:
                    tile(2 * j, 0, j)
                    tile(2 * j + 1, 1, j)
                tile(TILES - 3, 0, last)
                tile(TILES - 2, 1, last, False)
                turn_h(TILES - 1, 0, TILES)
                turn_p(TILES - 1, 0, last + 1)
                second(TILES - 1)
                middle(TILES - 1)

            def high(eng, kind, t):
                eng.wait_ge(s[f"{kind}_t"], after(t + 1))
                eng.wait_ge(s[{"o": "f_ready", "p": "p_ready", "h": "g_ready"}[kind]], after(t))
                nc.scalar.activation(hi[kind][:, :, :], bank[kind][:, 0:KS[kind] * P], ACT.Copy).then_inc(s[f"{kind}_hi"], 1)

            def low(eng, kind, t):
                eng.wait_ge(s[f"{kind}_hi"], after(t + 1))
                eng.wait_ge(s[{"o": "f_ready", "p": "p_ready", "h": "g_ready"}[kind]], after(t))
                nc.vector.tensor_tensor(lo[kind][:, :, :],
                                        bank[kind][:, 0:KS[kind] * P].rearrange("p (k n) -> p k n", n=P),
                                        hi[kind][:, :, :].bitcast(F32), ALU.subtract).then_inc(s[f"{kind}_lo"], 1)

            @block.scalar
            def _(act):
                def squares(t):
                    act.wait_ge(s["o_in"], after(16 * t + 16))
                    act.wait_ge(s["ms_done"], after(t))
                    nc.scalar.activation(sq[:, :], ot[:, :], ACT.Square).then_inc(s["squared"], 1)

                def tanhs(t):
                    act.wait_ge(s["g_ready"], after(t + 1))
                    act.wait_ge(s["out_done"], after(t))
                    nc.scalar.activation(expo[:, :], ps_g[:, :], ACT.Tanh, scale=0.5).then_inc(s["e_done"], 1)

                for i, (n, k) in enumerate(loads):
                    if i == SCALE_AT:
                        squares(0)
                    if i == PART_AT:
                        high(act, "o", 0)
                    if i == NEXT_AT:
                        squares(1)
                    act.wait_ge(w_in[i % STAGES], after(16 * (i // STAGES + 1)))
                    nc.scalar.activation(w_hi[n][:, k, :], stage[i % STAGES][:, :], ACT.Copy).then_inc(s["w_hi_done"], 1)
                high(act, "o", 1)
                with act.Fori(0, TILES - 2) as t:
                    high(act, "h", t)
                    squares(t + 2)
                    high(act, "p", t)
                    high(act, "o", t + 2)
                    tanhs(t)
                for t in range(TILES - 2, TILES):
                    high(act, "h", t)
                    high(act, "p", t)
                    tanhs(t)

            @block.gpsimd
            def _(pool):
                def root_mean_square(t):
                    pool.wait_ge(s["ms_eps"], after(t + 1))
                    nc.gpsimd.tensor_tensor(ms[:, :], ms[:, :], core.minus_half[:, 0:heads],
                                            ALU.pow).then_inc(s["rms_done"], 1)

                def deviation(t):
                    pool.wait_ge(s["norm_eps"], after(t + 1))
                    nc.gpsimd.tensor_tensor(rstd[:, :], rstd[:, :], core.minus_half[:, 0:1],
                                            ALU.pow).then_inc(s["rstd_done"], 1)

                root_mean_square(0)
                root_mean_square(1)
                deviation(0)
                with pool.Fori(0, TILES - 2) as t:
                    root_mean_square(t + 2)
                    deviation(t + 1)
                deviation(TILES - 1)

            @block.vector
            def _(dve):
                def scale_heads(t):
                    by_head = ot[:, :].rearrange("p (h n) -> p h n", h=heads)
                    dve.wait_ge(s["squared"], after(t + 1))
                    dve.wait_ge(s["o_normed"], after(t))
                    nc.vector.reduce_sum(ms[:, :], sq[:, :].rearrange("p (h n) -> p h n", h=heads),
                                         AX.X).then_inc(s["ms_done"], 1)
                    dve.wait_ge(s["ms_done"], after(t + 1))
                    nc.vector.tensor_scalar(ms[:, :], ms[:, :], heads / D, EPS, ALU.mult,
                                            ALU.add).then_inc(s["ms_eps"], 1)
                    dve.wait_ge(s["rms_done"], after(t + 1))
                    nc.vector.tensor_tensor(by_head, by_head, ms[:, :].rearrange("p (h a) -> p h a", a=1)
                                            .broadcast_to([P, heads, D // heads]), ALU.mult).then_inc(s["o_normed"], 1)
                    dve.wait_ge(s["o_normed"], after(t + 1))
                    dve.wait_ge(s["f_in"], after(16 * t + 16))
                    nc.vector.tensor_tensor(ot[:, :], ot[:, :], ft[:, :], ALU.mult).then_inc(s["o_scaled"], 1)

                def norm(t, u, two_back):
                    dve.wait_ge(s["f_ready"], after(t + 1))
                    dve.wait_ge(s["x_in"], after(16 * t + 16))
                    if two_back:
                        dve.wait_ge(s["out_done"], after(t - 1))
                    nc.vector.scalar_tensor_tensor(h[u][:, :], xt[:, :], ALPHA, ps_f[:, :], ALU.mult,
                                                   ALU.add).then_inc(s["y_done"], 1)
                    dve.wait_ge(s["y_done"], after(t + 1))
                    for half in range(2):
                        ins = nc.vector.bn_stats(stats[:, half, :], h[u][:, half * BANK:(half + 1) * BANK])
                    ins.then_inc(s["norm_stat"], 1)
                    dve.wait_ge(s["norm_stat"], after(t + 1))
                    stand_alone(dve, core)
                    nc.vector.bn_aggr(mv[:, :], stats[:, :, :]).then_inc(s["norm_mv"], 1)
                    dve.wait_ge(s["norm_mv"], after(t + 1))
                    dve.wait_ge(s["h_norm"], after(t))
                    nc.vector.tensor_scalar(rstd[:, :], mv[:, 1:2], EPS, None, ALU.add).then_inc(s["norm_eps"], 1)
                    dve.wait_ge(s["rstd_done"], after(t + 1))
                    nc.vector.tensor_scalar(h[u][:, :], h[u][:, :], mv[:, 0:1], rstd[:, :], ALU.subtract,
                                            ALU.mult).then_inc(s["h_norm"], 1)
                    dve.wait_ge(s["h_norm"], after(t + 1))
                    nc.vector.tensor_tensor(h[u][:, :], h[u][:, :], gb[:, :], ALU.mult).then_inc(s["h_scaled"], 1)
                    dve.wait_ge(s["h_scaled"], after(t + 1))
                    nc.vector.tensor_tensor(h[u][:, :], h[u][:, :], bb[:, :], ALU.add).then_inc(s["h_done"], 1)

                def gate(t, u):
                    dve.wait_ge(s["e_done"], after(t + 1))
                    dve.wait_ge(s["p_ready"], after(t + 1))
                    nc.vector.scalar_tensor_tensor(expo[:, :], expo[:, :], 1.0, ps_p[:, :], ALU.add,
                                                   ALU.mult).then_inc(s["e_mul"], 1)
                    dve.wait_ge(s["e_mul"], after(t + 1))
                    dve.wait_ge(s["stored"], after(16 * t))
                    nc.vector.scalar_tensor_tensor(out[:, :], expo[:, :], 0.5, h[u][:, :], ALU.mult,
                                                   ALU.add).then_inc(s["out_done"], 1)

                def tile(t, u, two_back=True, more=True):
                    low(dve, "h", t)
                    if more:
                        scale_heads(t + 2)
                    low(dve, "p", t)
                    if more:
                        low(dve, "o", t + 2)
                    norm(t + 1, 1 - u, two_back)
                    gate(t, u)

                for i, (n, k) in enumerate(loads):
                    if i == SCALE_AT:
                        scale_heads(0)
                    if i == PART_AT:
                        low(dve, "o", 0)
                    if i == NEXT_AT:
                        scale_heads(1)
                    dve.wait_ge(s["w_hi_done"], after(i + 1))
                    nc.vector.tensor_tensor(w_lo[n][:, k, :], stage[i % STAGES][:, :], w_hi[n][:, k, :].bitcast(F32),
                                            ALU.subtract).then_inc(s["w_lo_done"], 1)
                dve.wait_ge(s["w_lo_done"], after(len(loads)))
                dve.wait_ge(s["rows_in"], after(32))
                low(dve, "o", 1)
                norm(0, 0, False)
                tile(0, 0, two_back=False)
                with dve.Fori(0, TILES // 2 - 1) as j:
                    tile(2 * j + 1, 1)
                    tile(2 * j + 2, 0)
                tile(TILES - 2, 1, more=False)
                low(dve, "h", TILES - 1)
                low(dve, "p", TILES - 1)
                gate(TILES - 1, 0)


def key_pieces(n):
    ends = list(range(n, 0, -BANK))
    return [(max(0, e - BANK), e) for e in reversed(ends)]


def attention(core, q, k, v, rev, rel_bias, o):
    nc = core.nc
    T = PROMPT_TILES
    NEAR = 2 * P
    pieces = [key_pieces((i + 1) * P) for i in range(T)]
    first_piece = [2 * sum(len(pieces[a]) for a in range(i)) for i in range(T + 1)]
    groups = [-(-(i + 1) // 4) for i in range(T)]
    first_group = [sum(groups[:i]) for i in range(T + 1)]
    PIECES, GROUPS, PREPS = first_piece[T], first_group[T], 16
    RING = 4
    preps = [(is_q, m, g) for g in range(4) for m in range(2) for is_q in (False, True)]
    beside = [1] * T
    with ExitStack() as mem:
        def sb(name, shape, dt=F32):
            return mem.enter_context(nc.sbuf_tensor(f"att_{name}", shape, dt))

        def ps(name):
            return mem.enter_context(nc.psum_tensor(f"att_{name}", [P, BANK], F32))

        k_nat = sb("k_nat", [P, T, 2, 2, D_DH])
        q_nat = sb("q_nat", [P, T, 2, 2, D_DH])
        v_sb = [sb(f"v{u}", [P, T, D_VD]) for u in range(2)]
        bias = [sb(f"bias{u}", [P, NEAR]) for u in range(2)]
        far = [sb(f"far{u}", [P, 1]) for u in range(2)]
        k_hi = [[sb(f"k_hi{u}{m}", [P, SEQ], F32R) for m in range(2)] for u in range(2)]
        k_lo = [[sb(f"k_lo{u}{m}", [P, SEQ], F32R) for m in range(2)] for u in range(2)]
        q_hl = [[sb(f"q_hl{u}{m}", [P, SEQ], F32R) for m in range(2)] for u in range(2)]
        s_sb = [sb(f"s{i}", [P, 2, SEQ]) for i in range(2)]
        a = [sb(f"a{i}", [P, SEQ]) for i in range(2)]
        a_t = [sb(f"a_t{i}", [P, BANK]) for i in range(2)]
        mx = sb("mx", [P, 2, 8])
        top = sb("top", [P, 2])
        neg = [sb(f"neg{i}", [P, 2]) for i in range(2)]
        total = [sb(f"total{i}", [P, 2]) for i in range(2)]
        inv = [sb(f"inv{i}", [P, 2]) for i in range(2)]
        weight = sb("weight", [P, 1])
        o_sb = [sb(f"o{i}", [P, D_VD]) for i in range(2)]
        ps_s = [ps(f"ps_s{i}") for i in range(RING)]
        ps_k = ps("ps_k")
        ps_a = [ps(f"ps_a{i}") for i in range(2)]
        ps_o = ps("ps_o")

        turn_banks = [ps_k] + ps_a

        s = {n: core.sem(f"att_{n}") for n in
             ("turned hi_done lo_done piece_ready piece_free max_done neg_done exp_done inv_done "
              "weight_done a_done a_turned a_copied a_met o_copied").split()}
        nat_in = [core.sem(f"att_nat_in{g}") for g in range(4)]
        head_in = [core.sem(f"att_head_in{u}") for u in range(2)]
        stored = [core.sem(f"att_stored{i}") for i in range(2)]

        def ahead(H, u, i, by):
            return (H, u, i + by) if i + by < T else (H + 1, 1 - u, i + by - T)

        def over_heads(eng, head):
            with eng.Fori(0, D_HEADS // 2 - 1) as j:
                head(2 * j, 0, False)
                head(2 * j + 1, 1, False)
            head(D_HEADS - 2, 0, False)
            head(D_HEADS - 1, 1, True)

        def slots(i):
            start = sum(beside[:i])
            return preps[start:start + beside[i]], start

        core.begin()
        with nc.Block() as block:

            @block.sync
            def _(sp):
                def tiled(ap, h):
                    return ap[0:SEQ, bass.ds(h * D_VD, D_VD)].rearrange("(t p) d -> p t d", p=P)

                def load_nat(h, g):
                    for nat, src in ((k_nat, k), (q_nat, q)):
                        for side in range(2):
                            for m in range(2):
                                sp.dma_start(nat[:, 4 * g:4 * g + 4, m, side, :],
                                             src[g * BANK:(g + 1) * BANK, bass.ds(h * D_VD + m * D_DH, D_DH)]
                                             .rearrange("(t p) d -> p t d", p=P)).then_inc(nat_in[g], 16)

                def load_head(h, u):
                    sp.dma_start(v_sb[u][:, :, :], tiled(v, h)).then_inc(head_in[u], 16)
                    sp.dma_start(bias[u][:, :], bias_view(rev, h)).then_inc(head_in[u], 16)
                    sp.dma_start(far[u][:, :], rel_bias[N_BUCKETS - 1:N_BUCKETS, bass.ds(h, 1)]
                                 .broadcast_to([P, 1])).then_inc(head_in[u], 16)

                for g in range(4):
                    load_nat(0, g)
                load_head(0, 0)
                for g in range(4):
                    sp.wait_ge(s["turned"], after(4 * g + 4))
                    load_nat(1, g)

                def head(H, u, last):
                    if not last:
                        sp.wait_ge(s["o_copied"], after(T * H))
                        stand_alone(sp, core)
                        sp.wait_ge(s["piece_ready"], after(PIECES * H))
                        stand_alone(sp, core)
                        load_head(H + 1, 1 - u)
                    for i in range(T):
                        sp.wait_ge(s["o_copied"], after(T * H + i + 1))
                        stand_alone(sp, core)
                        sp.dma_start(o[i * P:(i + 1) * P, bass.ds(H * D_VD, D_VD)],
                                     o_sb[i % 2][:, :]).then_inc(stored[i % 2], 16)
                        if i % 4 == 3 and not (isinstance(H, int) and H + 2 >= D_HEADS):
                            sp.wait_ge(s["turned"], after(PREPS * (H + 1) + i + 1))
                            stand_alone(sp, core)
                            load_nat(H + 2, i // 4)

                over_heads(sp, head)
                for i in range(2):
                    sp.wait_ge(stored[i], after(16 * D_HEADS * T // 2))

            @block.tensor
            def _(pe):
                def prep(H, n, is_q, m, g, banks=turn_banks[:1]):
                    if n % 4 == 0:
                        pe.wait_ge(nat_in[n // 4], after(128 * (H + 1)))
                    if len(banks) == 1 or n >= len(banks):
                        pe.wait_ge(s["hi_done"], after(PREPS * H + n + 1 - len(banks)))
                        pe.wait_ge(s["lo_done"], after(PREPS * H + n + 1 - len(banks)))
                    src = q_nat if is_q else k_nat
                    for b in range(4):
                        mm = nc.tensor.transpose(banks[n % len(banks)][:, b * P:(b + 1) * P],
                                                 src[:, 4 * g + b, m, :, :].rearrange("p a d -> p (a d)"),
                                                 core.ident[:, :])
                    mm.then_inc(s["turned"], 1)

                def scores(H, u, i):
                    for m in range(2):
                        for c, (lo_, hi_) in enumerate(pieces[i]):
                            n = first_piece[i] + m * len(pieces[i]) + c
                            if m == 0 and c == 0:
                                need = 4 * (i // 4 + 1)
                                pe.wait_ge(s["hi_done"], after(PREPS * H + need))
                                pe.wait_ge(s["lo_done"], after(PREPS * H + need))
                            pe.wait_ge(s["piece_free"], after(PIECES * H + n + 1))
                            dst = ps_s[n % RING][:, 0:hi_ - lo_]
                            lhs = q_hl[u][m][:, i * P:(i + 1) * P]
                            nc.tensor.matmul(dst, lhs, k_hi[u][m][:, lo_:hi_], start=True, stop=False)
                            nc.tensor.matmul(dst, lhs, k_lo[u][m][:, lo_:hi_], start=False,
                                             stop=True).then_inc(s["piece_ready"], 1)
                            yield

                def turn(H, i, g):
                    if g == 0:
                        pe.wait_ge(s["a_done"], after(T * H + i + 1))
                    n = first_group[i] + g
                    if n >= 2:
                        pe.wait_ge(s["a_copied"], after(GROUPS * H + n - 1))
                    for b in range(4 * g, min(4 * g + 4, i + 1)):
                        mm = nc.tensor.transpose(ps_a[n % 2][:, (b % 4) * P:(b % 4 + 1) * P],
                                                 a[i % 2][:, b * P:(b + 1) * P], core.ident[:, :])
                    mm.then_inc(s["a_turned"], 1)

                def meet(H, u, i, g):
                    n = first_group[i] + g
                    if i == 0:
                        pe.wait_ge(head_in[u], after(48 * (H // 2 + 1) if isinstance(H, int) else 24 * (H - u) + 48))
                    if g == 0:
                        pe.wait_ge(s["o_copied"], after(T * H + i))
                    pe.wait_ge(s["a_copied"], after(GROUPS * H + n + 1))
                    for b in range(4 * g, min(4 * g + 4, i + 1)):
                        mm = nc.tensor.matmul(ps_o[:, 0:D_VD], a_t[n % 2][:, (b % 4) * P:(b % 4 + 1) * P],
                                              v_sb[u][:, b, :], start=(b == 0), stop=(b == i))
                    mm.then_inc(s["a_met"], 1)

                def values(H, u, i):
                    for g in range(groups[i] + 2):
                        if g >= 2:
                            meet(H, u, i, g - 2)
                        if g < groups[i]:
                            turn(H, i, g)
                        if g >= 1:
                            yield

                def head(H, u, last):
                    for i in range(T):
                        todo = [] if last else list(enumerate(slots(i)[0]))
                        for n, (is_q, m, g) in todo[:1]:
                            prep(H + 1, slots(i)[1] + n, is_q, m, g)
                        mixed = values(H, u, i)
                        if not (last and i + 2 >= T):
                            ahead_to = ahead(H, u, i, 2)
                            for step, _ in enumerate(scores(*ahead_to), 1):
                                if step >= RING and step % 2 == 0:
                                    next(mixed, None)
                        for _ in mixed:
                            pass
                        for n, (is_q, m, g) in todo[1:]:
                            prep(H + 1, slots(i)[1] + n, is_q, m, g)

                for n, (is_q, m, g) in enumerate(preps):
                    prep(0, n, is_q, m, g, turn_banks)
                for i in range(2):
                    for _ in scores(0, 0, i):
                        pass
                over_heads(pe, head)

            @block.scalar
            def _(act):
                def high(H, u, n, is_q, m, g, banks=turn_banks[:1]):
                    act.wait_ge(s["turned"], after(PREPS * H + n + 1))
                    dst = (q_hl if is_q else k_hi)[u][m]
                    nc.scalar.activation(dst[:, g * BANK:(g + 1) * BANK], banks[n % len(banks)][:, :], ACT.Copy,
                                         scale=D_DH ** -0.5 if is_q else 1.0).then_inc(s["hi_done"], 1)

                def exps(H, u, i, m):
                    n = (i + 1) * P
                    act.wait_ge(s["neg_done"], after(T * H + i + 1))
                    nc.scalar.activation(s_sb[i % 2][:, m, 0:n], s_sb[i % 2][:, m, 0:n], ACT.Exp,
                                         bias=neg[i % 2][:, m:m + 1],
                                         accum_out=total[i % 2][:, m:m + 1]).then_inc(s["exp_done"], 1)

                def copies(H, i, from_, to):
                    for g in range(from_, min(to, groups[i])):
                        n = first_group[i] + g
                        act.wait_ge(s["a_turned"], after(GROUPS * H + n + 1))
                        if n >= 2:
                            act.wait_ge(s["a_met"], after(GROUPS * H + n - 1))
                        cols = P * (min(4 * g + 4, i + 1) - 4 * g)
                        nc.scalar.activation(a_t[n % 2][:, 0:cols], ps_a[n % 2][:, 0:cols],
                                             ACT.Copy).then_inc(s["a_copied"], 1)

                def output(H, i):
                    act.wait_ge(s["a_met"], after(GROUPS * H + first_group[i + 1]))
                    act.wait_ge(stored[i % 2], after(16 * (T // 2 * H + i // 2)))
                    nc.scalar.activation(o_sb[i % 2][:, :], ps_o[:, 0:D_VD], ACT.Copy,
                                         scale=inv[i % 2][:, 0:1]).then_inc(s["o_copied"], 1)

                def head(H, u, last):
                    for i in range(T):
                        todo = [] if last else list(enumerate(slots(i)[0]))
                        for n, (is_q, m, g) in todo[:1]:
                            high(H + 1, 1 - u, slots(i)[1] + n, is_q, m, g)
                        more = not (last and i + 1 >= T)
                        if more:
                            exps(*ahead(H, u, i, 1), 0)
                        copies(H, i, 0, 2)
                        if more:
                            exps(*ahead(H, u, i, 1), 1)
                        copies(H, i, 2, groups[i])
                        output(H, i)
                        for n, (is_q, m, g) in todo[1:]:
                            high(H + 1, 1 - u, slots(i)[1] + n, is_q, m, g)

                for n, (is_q, m, g) in enumerate(preps):
                    high(0, 0, n, is_q, m, g, turn_banks)
                for m in range(2):
                    exps(0, 0, 0, m)
                over_heads(act, head)

            @block.vector
            def _(dve):
                def low(H, u, n, is_q, m, g, banks=turn_banks[:1]):
                    bank = banks[n % len(banks)]
                    dve.wait_ge(s["hi_done"], after(PREPS * H + n + 1))
                    cols = slice(g * BANK, (g + 1) * BANK)
                    if is_q:
                        part = q_hl[u][m][64:P, cols]
                        ins = nc.vector.scalar_tensor_tensor(part, bank[64:P, :], D_DH ** -0.5, part.bitcast(F32),
                                                             ALU.mult, ALU.subtract)
                    else:
                        ins = nc.vector.tensor_tensor(k_lo[u][m][:, cols], bank[:, :],
                                                      k_hi[u][m][:, cols].bitcast(F32), ALU.subtract)
                    ins.then_inc(s["lo_done"], 1)

                def take(H, u, i):
                    if i == 0:
                        dve.wait_ge(head_in[u], after(48 * (H // 2 + 1) if isinstance(H, int) else 24 * (H - u) + 48))
                    if not (isinstance(H, int) and H == 0 and i == 0):
                        dve.wait_ge(s["a_done"], after(T * H + i - 1))
                    n_keys = (i + 1) * P
                    near = max(0, n_keys - NEAR)
                    for m in range(2):
                        col = 0
                        for c, (lo_, hi_) in enumerate(pieces[i]):
                            n = first_piece[i] + m * len(pieces[i]) + c
                            dve.wait_ge(s["piece_ready"], after(PIECES * H + n + 1))
                            if m == 0 and c == 0:
                                dve.wait_ge(s["max_done"], after(T * H + i))
                            cut = min(hi_, near)
                            if cut > lo_:
                                ins = nc.vector.tensor_scalar(s_sb[i % 2][:, m, lo_:cut],
                                                              ps_s[n % RING][:, 0:cut - lo_], far[u][:, :], None,
                                                              ALU.add, ALU.max, accum_out=mx[:, m, col:col + 1])
                                col += 1
                            if hi_ > near:
                                start = max(lo_, near)
                                if cut <= lo_:
                                    stand_alone(dve, core)
                                ins = nc.vector.tensor_tensor_reduce(
                                    out=s_sb[i % 2][:, m, start:hi_], in0=ps_s[n % RING][:, start - lo_:hi_ - lo_],
                                    in1=bias[u][:, NEAR - (n_keys - start):NEAR], scale=1.0, scalar=-3.0e38,
                                    op0=ALU.add, op1=ALU.max, accum_out=mx[:, m, col:col + 1])
                                col += 1
                            ins.then_inc(s["piece_free"], 1)
                    dve.wait_ge(s["piece_free"], after(PIECES * H + first_piece[i + 1] + RING))
                    nc.vector.reduce_max(top[:, :], mx[:, :, 0:col], AX.X).then_inc(s["max_done"], 1)
                    dve.wait_ge(s["max_done"], after(T * H + i + 1))
                    nc.vector.tensor_scalar(neg[i % 2][:, :], top[:, :], -1.0, None, ALU.mult).then_inc(s["neg_done"], 1)

                def combine(H, u, i):
                    n = (i + 1) * P
                    dve.wait_ge(s["exp_done"], after(2 * (T * H + i + 1)))
                    if i >= 2:
                        dve.wait_ge(s["o_copied"], after(T * H + i - 1))
                    nc.vector.reciprocal(inv[i % 2][:, :], total[i % 2][:, :]).then_inc(s["inv_done"], 1)
                    dve.wait_ge(s["inv_done"], after(T * H + i + 1))
                    nc.vector.scalar_tensor_tensor(weight[:, :], total[i % 2][:, 0:1], core.neg_lambda[:, :],
                                                   inv[i % 2][:, 1:2], ALU.mult, ALU.mult).then_inc(s["weight_done"], 1)
                    dve.wait_ge(s["weight_done"], after(T * H + i + 1))
                    dve.wait_ge(s["a_turned"], after(GROUPS * H + first_group[max(i - 1, 0)]))
                    nc.vector.scalar_tensor_tensor(a[i % 2][:, 0:n], s_sb[i % 2][:, 1, 0:n], weight[:, :],
                                                   s_sb[i % 2][:, 0, 0:n], ALU.mult, ALU.add).then_inc(s["a_done"], 1)

                def head(H, u, last):
                    for i in range(T):
                        if not (last and i + 1 >= T):
                            take(*ahead(H, u, i, 1))
                        combine(H, u, i)
                        if not last:
                            for n, (is_q, m, g) in enumerate(slots(i)[0]):
                                low(H + 1, 1 - u, slots(i)[1] + n, is_q, m, g)

                dve.sem_inc(s["piece_free"], RING)
                for n, (is_q, m, g) in enumerate(preps):
                    low(0, 0, n, is_q, m, g, turn_banks)
                take(0, 0, 0)
                over_heads(dve, head)


def bias_view(rev, h):
    flat = rev.rearrange("h r m -> h (r m)")
    return flat[bass.ds(h, 1), P - 1:P - 1 + P * (REV - 1)].rearrange("a (r m) -> (a r) m", m=REV - 1)[:, 0:2 * P]


def sample_attention(core, q, k, v, cache_k, cache_v, page_table, rev, rel_bias, o):
    nc = core.nc
    B, Q, H = DEC_BATCH, DEC_SEQ, D_HEADS
    HQ = H * Q
    KEYS = PAST + Q
    NEAR0 = PAST - PAGE
    RING = 4
    with ExitStack() as mem:
        def sb(name, shape, dt=F32):
            return mem.enter_context(nc.sbuf_tensor(f"smp_{name}", shape, dt))

        def ps(name, n=BANK):
            return mem.enter_context(nc.psum_tensor(f"smp_{name}", [P, n], F32))

        table = sb("table", [1, B * N_PAGES], I32)
        rows = {"q": sb("q_rows", [SAMPLE_ROWS, D]), "k": sb("k_rows", [SAMPLE_ROWS, D])}
        turned = {"q": sb("q_turned", [P, H, SAMPLE_ROWS]), "k": sb("k_turned", [P, H, SAMPLE_ROWS])}
        bias = sb("bias", [P, PAGE + Q])
        far = sb("far", [P, 1])
        comb = sb("comb", [P, HQ])
        comb2 = sb("comb2", [P, HQ])
        k_pg = [sb(f"k_pg{i}", [P, D]) for i in range(RING)]
        v_pg = [sb(f"v_pg{u}", [P, N_PAGES, D]) for u in range(2)]
        v_new = [sb(f"v_new{u}", [Q, D]) for u in range(2)]
        q_bd = [sb(f"q_bd{u}", [P, H, P]) for u in range(2)]
        k_new = [sb(f"k_new{u}", [P, H, Q]) for u in range(2)]
        k_t = [sb(f"k_t{i}", [P, H, PAGE]) for i in range(2)]
        p = [sb(f"p{u}", [P, KEYS]) for u in range(2)]
        mx = sb("mx", [P, 4])
        neg = sb("neg", [P, 1])
        total = sb("total", [P, 1])
        inv = sb("inv", [P, 1])
        comb_b = [sb(f"comb_b{u}", [P, HQ]) for u in range(2)]
        a_t = sb("a_t", [P, N_PAGES, HQ])
        a_new = sb("a_new", [Q, HQ])
        o_sb = sb("o_sb", [HQ, D])
        PAD = ROWS - SEQ - SAMPLE_ROWS
        zeros = sb("zeros", [PAD, D])
        ps_k = [ps(f"ps_k{i}") for i in range(2)]
        ps_s, ps_n, ps_a, ps_o = ps("ps_s", 2 * BANK), ps("ps_n"), ps("ps_a"), ps("ps_o", D)

        s = {n: core.sem(f"smp_{n}") for n in
             ("table_in rows_in bias_in masks cleared row_turned row_copied comb_done ready_qk k_turned0 k_turned1 "
              "k_copied0 k_copied1 s_ready s_new_ready taken max_done neg_done exp_done inv_done comb_ready "
              "a_turned a_copied a_new_copied o_ready o_copied stored").split()}
        k_in = [core.sem(f"smp_k_in{i}") for i in range(RING)]
        v_in = [core.sem(f"smp_v_in{u}") for u in range(2)]

        masks = 2 * 2 + 2 + 1

        core.begin()
        with nc.Block() as block:

            @block.sync
            def _(sp):
                sp.dma_start(table[:, :], page_table.rearrange("b n -> (b n)").rearrange("(a n) -> a n", a=1)
                             ).then_inc(s["table_in"], 16)
                for name, src in (("q", q), ("k", k)):
                    sp.dma_start(rows[name][:, :], src[SEQ:SEQ + SAMPLE_ROWS, :]).then_inc(s["rows_in"], 16)
                sp.wait_ge(s["table_in"], after(16))

                def page_of(b, pg):
                    return sp.value_load(table[0:1, bass.ds(b * N_PAGES + pg, 1)], min_val=0, max_val=N_POOL - 1)

                def key_page(b, pg, first):
                    page = page_of(b, pg)
                    if not (first and pg < RING):
                        sp.wait_ge(s["k_turned1"], after(N_PAGES * b + pg - RING + 1))
                    sp.dma_start(k_pg[pg % RING][:, :], cache_k[bass.ds(page, 1)]
                                 .rearrange("a p n -> (a p) n")).then_inc(k_in[pg % RING], 16)

                def value_page(b, u, pg):
                    page = page_of(b, pg)
                    sp.dma_start(v_pg[u][:, pg, :], cache_v[bass.ds(page, 1)]
                                 .rearrange("a p n -> (a p) n")).then_inc(v_in[u], 16)

                def load_bias():
                    for h in range(H):
                        for m in range(2):
                            at = 2 * Q * h + Q * m
                            sp.dma_start(bias[at:at + Q, :],
                                         bias_view(rev, h)[0:Q, 0:PAGE + Q]).then_inc(s["bias_in"], 16)
                        sp.dma_start(far[2 * Q * h:2 * Q * (h + 1), :], rel_bias[N_BUCKETS - 1:N_BUCKETS, h:h + 1]
                                     .broadcast_to([2 * Q, 1])).then_inc(s["bias_in"], 16)

                def sample(b, u, first):
                    for pg in range(N_PAGES):
                        key_page(b, pg, first)
                        if pg == RING - 1 and first:
                            load_bias()
                        if pg >= RING:
                            if pg == RING and not first:
                                sp.wait_ge(s["o_ready"], after(b - 1))
                                stand_alone(sp, core)
                            for n in (2 * (pg - RING), 2 * (pg - RING) + 1):
                                value_page(b, u, n)
                    sp.dma_start(v_new[u][:, :], v[bass.ds(b * Q + SEQ, Q), :]).then_inc(v_in[u], 16)

                def store(b):
                    sp.wait_ge(s["o_copied"], after(b + 1))
                    for h in range(H):
                        cols = slice(h * D_VD, (h + 1) * D_VD)
                        sp.dma_start(o[bass.ds(b * Q + SEQ, Q), cols],
                                     o_sb[h * Q:(h + 1) * Q, cols]).then_inc(s["stored"], 16)

                sample(0, 0, True)
                sample(1, 1, False)
                with sp.Fori(0, B // 2 - 1) as j:
                    sample(2 * j + 2, 0, False)
                    store(2 * j)
                    sample(2 * j + 3, 1, False)
                    store(2 * j + 1)
                store(B - 2)
                store(B - 1)
                sp.wait_ge(s["masks"], after(masks))
                sp.dma_start(o[SEQ + SAMPLE_ROWS:ROWS, :], zeros[:, :]).then_inc(s["stored"], 16)
                sp.wait_ge(s["stored"], after(16 * (H * B + 1)))

            @block.gpsimd
            def _(pool):
                count = [0]

                def select(ap, op, fill, base, pattern, mult):
                    pool.wait_ge(s["masks"], after(count[0]))
                    nc.gpsimd.affine_select(out=ap, in_=ap, compare_op=op, fill=fill, base=base,
                                            pattern=pattern, channel_multiplier=mult).then_inc(s["masks"], 1)
                    count[0] += 1

                def fill(ap, value):
                    nc.gpsimd.memset(ap, value).then_inc(s["masks"], 1)
                    count[0] += 1

                for m, mat in enumerate((comb, comb2)):
                    fill(mat[:, :], 0.0)
                    select(mat[:, :].rearrange("p (h q) -> p h q", h=H), ALU.not_equal, 1.0, -Q * m,
                           [[-2 * Q, H], [-1, Q]], 1)
                fill(zeros[:, :], 0.0)
                for u in range(2):
                    fill(q_bd[u][:, :, :], 0.0)
                assert count[0] == masks

            @block.tensor
            def _(pe):
                pe.wait_ge(s["rows_in"], after(32))
                for n, name in enumerate(("q", "k")):
                    pe.wait_ge(s["row_copied"], after(n))
                    for h in range(H):
                        mm = nc.tensor.transpose(ps_k[0][:, h * SAMPLE_ROWS:(h + 1) * SAMPLE_ROWS],
                                                 rows[name][:, h * D_VD:(h + 1) * D_VD],
                                                 core.ident[0:SAMPLE_ROWS, 0:SAMPLE_ROWS])
                    mm.then_inc(s["row_turned"], 1)
                pe.wait_ge(s["row_copied"], after(2))
                pe.wait_ge(s["masks"], after(masks))

                def turn(b, pg):
                    n = N_PAGES * b + pg
                    pe.wait_ge(k_in[pg % RING], after(16 * (N_PAGES // RING * b + pg // RING + 1)))
                    for half in range(2):
                        pe.wait_ge(s[f"k_copied{half}"], after(n))
                        for i in range(H // 2):
                            h = half * (H // 2) + i
                            mm = nc.tensor.transpose(ps_k[half][:, i * P:(i + 1) * P],
                                                     k_pg[pg % RING][:, h * D_VD:(h + 1) * D_VD], core.ident[:, :])
                        mm.then_inc(s[f"k_turned{half}"], 1)

                def keys(b, u):
                    pe.wait_ge(s["ready_qk"], after(b + 1))
                    pe.wait_ge(s["taken"], after(b))
                    for pg in range(N_PAGES):
                        if pg + 1 < N_PAGES:
                            turn(b, pg + 1)
                        for half in range(2):
                            pe.wait_ge(s[f"k_copied{half}"], after(N_PAGES * b + pg + 1))
                        for h in range(H):
                            mm = nc.tensor.matmul(ps_s[:, pg * PAGE:(pg + 1) * PAGE], q_bd[u][:, h, :],
                                                  k_t[pg % 2][:, h, :], start=(h == 0), stop=(h == H - 1))
                        mm.then_inc(s["s_ready"], 1)
                    for h in range(H):
                        mm = nc.tensor.matmul(ps_n[:, 0:Q], q_bd[u][:, h, :], k_new[u][:, h, :],
                                              start=(h == 0), stop=(h == H - 1))
                    mm.then_inc(s["s_new_ready"], 1)

                def values(b, u, j, taken, following=None):
                    pe.wait_ge(s["comb_ready"], after(b + 1))
                    for pg in range(N_PAGES):
                        nc.tensor.matmul(ps_a[:, pg * HQ:(pg + 1) * HQ], p[u][:, pg * PAGE:(pg + 1) * PAGE],
                                         comb_b[u][:, :], start=True, stop=True)
                    pe.wait_ge(s["taken"], after(taken))
                    nc.tensor.matmul(ps_n[0:Q, HQ:2 * HQ], p[u][:, PAST:KEYS], comb_b[u][:, :], start=True,
                                     stop=True).then_inc(s["a_turned"], 1)
                    if following is not None:
                        turn(following, 0)
                    pe.wait_ge(s["a_copied"], after(b + 1))
                    pe.wait_ge(s["a_new_copied"], after(b + 1))
                    pe.wait_ge(v_in[u], after(16 * (N_PAGES + 1) * (j + 1)))
                    pe.wait_ge(s["o_copied"], after(b))
                    for half in range(2):
                        cols = slice(half * BANK, (half + 1) * BANK)
                        for pg in range(N_PAGES):
                            nc.tensor.matmul(ps_o[0:HQ, cols], a_t[:, pg, :], v_pg[u][:, pg, cols],
                                             start=(pg == 0), stop=False)
                        mm = nc.tensor.matmul(ps_o[0:HQ, cols], a_new[:, :], v_new[u][:, cols],
                                              start=False, stop=True)
                    mm.then_inc(s["o_ready"], 1)

                turn(0, 0)
                keys(0, 0)
                turn(1, 0)
                with pe.Fori(0, B // 2 - 1) as j:
                    keys(2 * j + 1, 1)
                    values(2 * j, 0, j, 2 * j + 2, 2 * j + 2)
                    keys(2 * j + 2, 0)
                    values(2 * j + 1, 1, j, 2 * j + 3, 2 * j + 3)
                keys(B - 1, 1)
                for b in (B - 2, B - 1):
                    values(b, b % 2, B // 2 - 1, B)

            @block.scalar
            def _(act):
                act.wait_ge(s["row_turned"], after(1))
                nc.scalar.activation(turned["q"][:, :, :], ps_k[0][:, 0:H * SAMPLE_ROWS], ACT.Copy,
                                     scale=D_DH ** -0.5).then_inc(s["row_copied"], 1)
                act.wait_ge(s["row_turned"], after(2))
                nc.scalar.activation(turned["k"][:, :, :], ps_k[0][:, 0:H * SAMPLE_ROWS],
                                     ACT.Copy).then_inc(s["row_copied"], 1)

                def pages(b, from_, to=N_PAGES):
                    for pg in range(from_, to):
                        n = N_PAGES * b + pg
                        act.wait_ge(s["k_turned0"], after(n + 1))
                        if pg >= 2:
                            act.wait_ge(s["s_ready"], after(n - 1))
                        nc.scalar.activation(k_t[pg % 2][:, 0:H // 2, :], ps_k[0][:, :],
                                             ACT.Copy).then_inc(s["k_copied0"], 1)

                def exps(b, u):
                    act.wait_ge(s["neg_done"], after(b + 1))
                    nc.scalar.activation(p[u][:, :], p[u][:, :], ACT.Exp, bias=neg[:, :],
                                         accum_out=total[:, :]).then_inc(s["exp_done"], 1)

                def turned_probs(b):
                    act.wait_ge(s["a_turned"], after(b + 1))
                    nc.scalar.activation(a_t[:, :, :], ps_a[:, :], ACT.Copy).then_inc(s["a_copied"], 1)

                def output(b):
                    act.wait_ge(s["o_ready"], after(b + 1))
                    act.wait_ge(s["stored"], after(16 * H * b))
                    nc.scalar.activation(o_sb[:, :], ps_o[0:HQ, :], ACT.Copy).then_inc(s["o_copied"], 1)

                pages(0, 0)
                exps(0, 0)
                pages(1, 0, 1)
                with act.Fori(0, B // 2 - 1) as j:
                    for u in range(2):
                        pages(2 * j + u + 1, 1)
                        exps(2 * j + u + 1, 1 - u)
                        turned_probs(2 * j + u)
                        pages(2 * j + u + 2, 0, 1)
                        output(2 * j + u)
                pages(B - 1, 1)
                exps(B - 1, 1)
                for b in (B - 2, B - 1):
                    turned_probs(b)
                    output(b)

            @block.vector
            def _(dve):
                dve.wait_ge(s["masks"], after(masks))
                nc.vector.scalar_tensor_tensor(comb[:, :], comb2[:, :], core.neg_lambda[:, :], comb[:, :],
                                               ALU.mult, ALU.add).then_inc(s["comb_done"], 1)
                dve.wait_ge(s["comb_done"], after(1))
                dve.wait_ge(s["row_copied"], after(2))

                def place(b, u, first):
                    if not first:
                        dve.wait_ge(s["s_new_ready"], after(b - 1))
                    for h in range(H):
                        for m in range(2):
                            half = slice(m * D_DH, (m + 1) * D_DH)
                            at = 2 * Q * h + Q * m
                            nc.vector.tensor_copy(q_bd[u][half, h, at:at + Q], turned["q"][half, h, bass.ds(b * Q, Q)])
                    nc.vector.tensor_copy(k_new[u][:, :, :],
                                          turned["k"][:, :, bass.ds(b * Q, Q)]).then_inc(s["ready_qk"], 1)

                def pages(b, from_, to=N_PAGES):
                    for pg in range(from_, to):
                        n = N_PAGES * b + pg
                        dve.wait_ge(s["k_turned1"], after(n + 1))
                        if pg >= 2:
                            dve.wait_ge(s["s_ready"], after(n - 1))
                        nc.vector.tensor_copy(k_t[pg % 2][:, H // 2:H, :], ps_k[1][:, :]).then_inc(s["k_copied1"], 1)

                def take(b, u, first):
                    dve.wait_ge(s["s_ready"], after(N_PAGES * (b + 1)))
                    dve.wait_ge(s["s_new_ready"], after(b + 1))
                    if not first:
                        dve.wait_ge(s["a_turned"], after(b - 1))
                    dve.wait_ge(s["max_done"], after(b))
                    for col, (lo_, hi_) in enumerate(((0, BANK), (BANK, NEAR0))):
                        nc.vector.tensor_scalar(p[u][:, lo_:hi_], ps_s[:, lo_:hi_], far[:, :], None,
                                                ALU.add, ALU.max, accum_out=mx[:, col:col + 1])
                    nc.vector.tensor_tensor_reduce(out=p[u][:, NEAR0:PAST], in0=ps_s[:, NEAR0:PAST],
                                                   in1=bias[:, 0:PAGE], scale=1.0, scalar=-3.0e38, op0=ALU.add,
                                                   op1=ALU.max, accum_out=mx[:, 2:3])
                    nc.vector.tensor_tensor_reduce(out=p[u][:, PAST:KEYS], in0=ps_n[:, 0:Q],
                                                   in1=bias[:, PAGE:PAGE + Q], scale=1.0, scalar=-3.0e38,
                                                   op0=ALU.add, op1=ALU.max, accum_out=mx[:, 3:4]
                                                   ).then_inc(s["taken"], 1)
                    dve.wait_ge(s["taken"], after(b + 1))
                    dve.wait_ge(s["exp_done"], after(b))
                    nc.vector.reduce_max(neg[:, :], mx[:, :], AX.X).then_inc(s["max_done"], 1)
                    dve.wait_ge(s["max_done"], after(b + 1))
                    nc.vector.tensor_scalar(neg[:, :], neg[:, :], -1.0, None, ALU.mult).then_inc(s["neg_done"], 1)
                    dve.wait_ge(s["exp_done"], after(b + 1))
                    nc.vector.reciprocal(inv[:, :], total[:, :]).then_inc(s["inv_done"], 1)
                    dve.wait_ge(s["inv_done"], after(b + 1))
                    nc.vector.tensor_scalar(comb_b[u][:, :], comb[:, :], inv[:, :], None,
                                            ALU.mult).then_inc(s["comb_ready"], 1)

                def finish(b):
                    dve.wait_ge(s["a_turned"], after(b + 1))
                    if not (isinstance(b, int) and b == 0):
                        dve.wait_ge(s["o_ready"], after(b))
                    nc.vector.tensor_copy(a_new[:, :], ps_n[0:Q, HQ:2 * HQ]).then_inc(s["a_new_copied"], 1)

                place(0, 0, True)
                pages(0, 0)
                dve.wait_ge(s["bias_in"], after(16 * 3 * H))
                take(0, 0, True)
                pages(1, 0, 1)
                place(1, 1, True)
                pages(1, 1)
                take(1, 1, True)
                finish(0)
                with dve.Fori(0, B // 2 - 1) as j:
                    for u in range(2):
                        pages(2 * j + 2 + u, 0, 1)
                        place(2 * j + 2 + u, u, False)
                        pages(2 * j + 2 + u, 1)
                        take(2 * j + 2 + u, u, False)
                        finish(2 * j + 1 + u)
                finish(B - 1)


def setup(core, lams, rel_bias, bucket_rows, rev):
    nc = core.nc

    def keep(name, shape):
        return core.ctx.enter_context(nc.sbuf_tensor(name, shape, F32))

    core.ident = keep("ident", [P, P])
    core.minus_half = keep("minus_half", [P, D_HEADS])
    core.neg_lambda = keep("neg_lambda", [P, 1])
    with ExitStack() as mem:
        lam = [mem.enter_context(nc.sbuf_tensor(f"lam{i}", [P, D_DH], F32)) for i in range(4)]
        dots = mem.enter_context(nc.sbuf_tensor("dots", [P, 2], F32))
        prod = mem.enter_context(nc.sbuf_tensor("prod", [P, D_DH], F32))
        table = mem.enter_context(nc.sbuf_tensor("bias_table", [N_BUCKETS + 1, D_HEADS], F32))
        pick = mem.enter_context(nc.sbuf_tensor("bias_pick", [N_BUCKETS + 1, REV], F32))
        row = mem.enter_context(nc.sbuf_tensor("bias_row", [D_HEADS, REV], F32))
        ps_row = mem.enter_context(nc.psum_tensor("ps_bias_row", [P, BANK], F32))
        loaded = core.sem("setup_loaded")
        made = core.sem("setup_made")
        dotted = core.sem("setup_dotted")
        raised = core.sem("setup_raised")
        lowered = core.sem("setup_lowered")
        picked = core.sem("setup_picked")
        copied = core.sem("setup_copied")
        stored = core.sem("setup_stored")
        core.begin()
        with nc.Block() as block:

            @block.sync
            def _(sp):
                for i in range(4):
                    sp.dma_start(lam[i][:, :], broadcast_row(lams[i], D_DH)).then_inc(loaded, 16)
                sp.dma_start(table[0:N_BUCKETS, :], rel_bias).then_inc(loaded, 16)
                sp.dma_start(pick[:, :], bucket_rows).then_inc(loaded, 16)
                sp.wait_ge(copied, after(1))
                sp.dma_start(rev, row[:, :].rearrange("h (a m) -> h a m", a=1).broadcast_to([D_HEADS, P, REV])
                             ).then_inc(stored, 16)
                sp.wait_ge(stored, after(16))

            @block.gpsimd
            def _(pool):
                nc.gpsimd.memset(core.ident[:, :], 0.0).then_inc(made, 1)
                nc.gpsimd.memset(core.minus_half[:, :], -0.5).then_inc(made, 1)
                pool.wait_ge(made, after(2))
                nc.gpsimd.memset(table[N_BUCKETS:N_BUCKETS + 1, :], 1.0).then_inc(made, 1)
                pool.wait_ge(made, after(3))
                nc.gpsimd.affine_select(out=core.ident[:, :], in_=core.ident[:, :], compare_op=ALU.not_equal,
                                        fill=1.0, base=0, pattern=[[-1, P]], channel_multiplier=1).then_inc(made, 1)

            @block.tensor
            def _(pe):
                pe.wait_ge(loaded, after(96))
                pe.wait_ge(made, after(4))
                nc.tensor.matmul(ps_row[0:D_HEADS, 0:REV], table[:, :], pick[:, :], start=True,
                                 stop=True).then_inc(picked, 1)

            @block.scalar
            def _(act):
                act.wait_ge(dotted, after(2))
                nc.scalar.activation(dots[:, :], dots[:, :], ACT.Exp).then_inc(raised, 1)

            @block.vector
            def _(dve):
                dve.wait_ge(loaded, after(96))
                for i in range(2):
                    dve.wait_ge(dotted, after(i))
                    nc.vector.tensor_tensor_reduce(out=prod[:, :], in0=lam[2 * i][:, :], in1=lam[2 * i + 1][:, :],
                                                   scale=1.0, scalar=0.0, op0=ALU.mult, op1=ALU.add,
                                                   accum_out=dots[:, i:i + 1]).then_inc(dotted, 1)
                dve.wait_ge(picked, after(1))
                nc.vector.tensor_copy(row[:, :], ps_row[0:D_HEADS, 0:REV]).then_inc(copied, 1)
                dve.wait_ge(raised, after(1))
                nc.vector.tensor_tensor(core.neg_lambda[:, :], dots[:, 1:2], dots[:, 0:1],
                                        ALU.subtract).then_inc(lowered, 1)
                dve.wait_ge(lowered, after(1))
                nc.vector.tensor_scalar(core.neg_lambda[:, :], core.neg_lambda[:, :], -LAM_INIT, None,
                                        ALU.add).then_inc(lowered, 1)


def decoder(nc, x, state, cache_k, cache_v, table, p, rel_bias, bucket_rows, w_gla, w_a2, b_a, g_gla, w_gla_out,
            w_diff, lq1, lk1, lq2, lk2, g_diff, w_diff_out, ln_g, ln_b, w_proj, w_gate,
            y, state_prompt, state_sample, k_out, v_out):
    def scratch(name, shape):
        return nc.dram_tensor(name, shape, F32, kind="Internal").ap()

    def halves(col, kind, dst, row=None, scale=1.0):
        out = []
        for a in range(0, D, BANK):
            extra = None if row is None else broadcast_row(row[a:a + BANK], BANK)
            out.append(([(col + a, col + a + BANK)], BANK, kind, dst[:, a:a + BANK], extra, scale))
        return out

    with ExitStack() as ctx:
        core = Core(nc, ctx)
        rev = scratch("bias_by_distance", [D_HEADS, P, REV])
        qka = scratch("gla_qka", [ROWS, 2 * GK + G_LOW])
        v = scratch("gla_v", [ROWS, GV])
        factors = scratch("factors", [ROWS, D])
        o = scratch("mixer_out", [ROWS, D])
        x1 = scratch("layer_out", [ROWS, D])
        q2 = scratch("diff_q", [ROWS, D])
        factors2 = scratch("factors2", [ROWS, D])
        o2 = scratch("mixer_out2", [ROWS, D])

        setup(core, [lq1[0], lk1[0], lq2[0], lk2[0]], rel_bias, bucket_rows, rev)
        core.end_phase()
        project(core, "vg", x, w_gla[0], halves(2 * GK, "copy", v)
                + halves(2 * GK + GV, "silu", factors, g_gla[0]))
        core.end_phase()
        third = (2 * GK + G_LOW) // 3
        low_rank = (2 * GK + 2 * GV, 2 * GK + 2 * GV + G_LOW)
        project(core, "qka", x, w_gla[0], [
            ([(0, third)], third, "copy", qka[:, 0:third], None, 1.0),
            ([(third, 2 * third)], third, "copy", qka[:, third:2 * third], None, 1.0),
            ([(2 * third, 2 * GK), low_rank], 2 * GK + G_LOW - 2 * third, "copy", qka[:, 2 * third:], None, 1.0)])
        core.end_phase()
        recurrence(core, qka, v, w_a2[0], b_a[0], o, state[0], state_prompt[0, 0], state_sample[0])
        core.end_phase()
        residual(core, "res1", x, o, G_HEADS, factors, p[0], w_gla_out[0], ln_g[0], ln_b[0], w_gate[0],
                 w_proj[0], x1)
        core.end_phase()
        project(core, "qk", x1, w_diff[0], halves(0, "copy", q2) + halves(D, "copy", k_out))
        core.end_phase()
        project(core, "vg2", x1, w_diff[0], halves(2 * D, "copy", v_out)
                + halves(3 * D, "silu", factors2, g_diff[0], 1.0 - LAM_INIT))
        core.end_phase()
        attention(core, q2, k_out, v_out, rev, rel_bias, o2)
        core.end_phase()
        sample_attention(core, q2, k_out, v_out, cache_k[0], cache_v[0], table, rev, rel_bias, o2)
        core.end_phase()
        residual(core, "res2", x1, o2, D_HEADS, factors2, p[1], w_diff_out[0], ln_g[1], ln_b[1], w_gate[1],
                 w_proj[1], y)


def bucket_table():
    distance = 2 * P - 1 - np.arange(REV)
    n = np.maximum(distance, 1).astype(np.float64)
    exact = N_BUCKETS // 2
    large = exact + (np.log(n / exact) / math.log(MAX_DISTANCE / exact) * (N_BUCKETS - exact)).astype(np.int32)
    bucket = np.where(distance < exact, np.maximum(distance, 0), np.minimum(large, N_BUCKETS - 1))
    pick = np.zeros((N_BUCKETS + 1, REV), np.float32)
    seen = distance >= 0
    pick[bucket[seen], np.nonzero(seen)[0]] = 1.0
    pick[N_BUCKETS, ~seen] = MASKED
    return pick


def rows_of(prompt, sample):
    lead, n = prompt.shape[:-3], prompt.shape[-1]
    parts = [prompt.reshape(*lead, SEQ, n), sample.reshape(*lead, SAMPLE_ROWS, n),
             np.zeros((*lead, ROWS - SEQ - SAMPLE_ROWS, n), prompt.dtype)]
    return np.concatenate(parts, axis=-2)


def kernel(**inputs):
    import concourse.bacc as bacc
    from concourse.bass_utils import run_bass_kernel_spmd as run

    nc = bacc.Bacc("TRN2", target_bir_lowering=False, num_devices=1)
    given = {n: np.asarray(a) for n, a in inputs.items()}
    arrays = {
        "x": rows_of(given["x_prompt"], given["x_sample"]),
        "state": given["state_gla"],
        "cache_k": given["cache_k"].reshape(1, N_POOL, PAGE, D),
        "cache_v": given["cache_v"].reshape(1, N_POOL, PAGE, D),
        "table": given["page_table"],
        "p": rows_of(given["p_prompt"], given["p_sample"]),
        "rel_bias": given["rel_bias"],
        "bucket_rows": bucket_table(),
    }
    for name in ("gla_w_in", "gla_w_a2", "gla_b_a", "gla_norm_g", "gla_w_out", "diff_w_in", "diff_lam_q1",
                 "diff_lam_k1", "diff_lam_q2", "diff_lam_k2", "diff_norm_g", "diff_w_out", "ln_g", "ln_b",
                 "ple_w_proj", "ple_w_gate"):
        arrays[name] = given[name]
    arrays = {f"in_{n}": np.ascontiguousarray(a) for n, a in arrays.items()}
    args = [nc.dram_tensor(n, a.shape, mybir.dt.from_np(a.dtype), kind="ExternalInput").ap()
            for n, a in arrays.items()]
    outs = {"out_y": (ROWS, D), "out_state_prompt": (1, 1, G_HEADS, G_DK, G_DV),
            "out_state_sample": (1, DEC_BATCH, G_HEADS, G_DK, G_DV), "out_k": (ROWS, D), "out_v": (ROWS, D)}
    args += [nc.dram_tensor(n, shape, F32, kind="ExternalOutput").ap() for n, shape in outs.items()]
    decoder(nc, *args)
    got = run(nc, [arrays], core_ids=[0]).results[0]
    heads = (D_HEADS, D_VD)

    def prompt(name, *tail):
        return got[name][0:SEQ].reshape(*tail)

    def sample(name, *tail):
        return got[name][SEQ:SEQ + SAMPLE_ROWS].reshape(*tail)

    return (prompt("out_y", 1, SEQ, D), sample("out_y", DEC_BATCH, DEC_SEQ, D),
            got["out_state_prompt"], got["out_state_sample"],
            prompt("out_k", 1, 1, SEQ, *heads), prompt("out_v", 1, 1, SEQ, *heads),
            sample("out_k", 1, DEC_BATCH, DEC_SEQ, *heads), sample("out_v", 1, DEC_BATCH, DEC_SEQ, *heads))
```
